# Optimizing a Trainium2 kernel written in Bass

```python
import math
import jax
import jax.numpy as jnp
from jax import lax
import numpy as np

D_MODEL = 1024
BATCH = 1
SEQ = 512
DEPTH = 2
DEC_BATCH = 1
DEC_SEQ = 256
PAST_LEN = 128

GRID_W = 64
HEAD_DIM = 64
D_MIX = D_MODEL
A_HEADS = 4
A_DIM = A_HEADS * HEAD_DIM
A_LORA_W = 32
A_LORA_A = 32
A_LORA_G = 64
B_HEADS = 8
B_DIM = B_HEADS * HEAD_DIM
NA_KH_MAX = 8
NA_KW = 16
C_DIM = D_MIX - A_DIM - B_DIM
C_GROUPS = C_DIM // HEAD_DIM
HY_ORDER = 2
HY_BANDS = 16
HY_EMB = 1 + 2 * HY_BANDS
HY_FF = 64
HY_FAST_DECAY_PCT = 0.3
HY_SLOW_DECAY_PCT = 1.5
HY_TARGET = 1e-2
D_FF = 2816
NORM_EPS = 1e-5
GN_EPS = 64e-5
A_COLS = 3 * A_DIM + 2 * A_LORA_W + 2 * A_LORA_A + A_LORA_G
B_COLS = 3 * B_DIM
C_COLS = (HY_ORDER + 1) * C_DIM
N_PROJ = A_COLS + B_COLS + C_COLS

kernel_name = 'hybrid_bidir_rwkv7_natten2d_hyena_encoder'

def rms_norm(x, g):
    xf = x.astype(jnp.float32)
    y = xf * lax.rsqrt(jnp.mean(xf * xf, axis=-1, keepdims=True) + NORM_EPS)
    return (y * g.astype(jnp.float32)).astype(x.dtype)

def group_rms_norm(x, g, n_groups):
    xf = x.astype(jnp.float32)
    xg = xf.reshape(xf.shape[:-1] + (n_groups, xf.shape[-1] // n_groups))
    y = xg * lax.rsqrt(jnp.mean(xg * xg, axis=-1, keepdims=True) + NORM_EPS)
    return y.reshape(xf.shape) * g.astype(jnp.float32)

def swiglu(x, w_in, w_out):
    gate, up = jnp.split(x @ w_in, 2, axis=-1)
    return (jax.nn.silu(gate) * up) @ w_out

def shift_prev(x):
    return jnp.pad(x, ((0, 0), (1, 0), (0, 0)))[:, :-1]

def shift_next(x):
    return jnp.pad(x, ((0, 0), (0, 1), (0, 0)))[:, 1:]

def wkv7_scan(r, decay, k, v, kk, a, reverse):
    bsz, _, n_h, n = r.shape

    def step(s, inp):
        r_t, w_t, k_t, v_t, kk_t, a_t = inp
        s = (s * w_t[:, :, None, :]
             - jnp.einsum('bhij,bhj->bhi', s, kk_t)[..., None] * (kk_t * a_t)[:, :, None, :]
             + v_t[..., None] * k_t[:, :, None, :])
        return s, jnp.einsum('bhij,bhj->bhi', s, r_t)

    xs = tuple(jnp.swapaxes(t, 0, 1) for t in (r, decay, k, v, kk, a))
    s0 = jnp.zeros((bsz, n_h, n, n), jnp.float32)
    _, o = lax.scan(step, s0, xs, reverse=reverse)
    return jnp.swapaxes(o, 0, 1)

def rwkv7_direction(r, decay, k, v, kk, a, r_k, ln_g, ln_b, reverse):
    o = wkv7_scan(r, decay, k, v, kk, a, reverse)
    mu = jnp.mean(o, axis=-1, keepdims=True)
    var = jnp.mean(jnp.square(o - mu), axis=-1, keepdims=True)
    o = (o - mu) * lax.rsqrt(var + GN_EPS) * ln_g + ln_b
    return o + jnp.sum(r * k * r_k, axis=-1, keepdims=True) * v

def rwkv7_mixer(p, lp):
    bsz, t_len, _ = p.shape
    p = p.astype(jnp.float32)
    p = p + lp['rwkv_mu'] * (0.5 * (shift_prev(p) + shift_next(p)) - p)
    cuts = [A_DIM, 2 * A_DIM, 3 * A_DIM, 3 * A_DIM + 2 * A_LORA_W,
            3 * A_DIM + 2 * A_LORA_W + 2 * A_LORA_A]
    r, k, v, wd, ad, gd = jnp.split(p, cuts, axis=-1)
    wd = wd.reshape(bsz, t_len, 2, A_LORA_W)
    ad = ad.reshape(bsz, t_len, 2, A_LORA_A)
    w_log = -jax.nn.softplus(-(lp['rwkv_w0'] + jnp.einsum('btdr,drc->btdc', jnp.tanh(wd), lp['rwkv_w_up']))) - 0.5
    decay = jnp.exp(-jnp.exp(w_log))
    a = jax.nn.sigmoid(lp['rwkv_a0'] + jnp.einsum('btdr,drc->btdc', ad, lp['rwkv_a_up']))
    g = jax.nn.sigmoid(gd) @ lp['rwkv_g_up']

    def heads(t):
        return t.reshape(t.shape[:-1] + (A_HEADS, HEAD_DIM))

    kk = heads(k * lp['rwkv_k_k'])
    kk = kk / jnp.maximum(jnp.sqrt(jnp.sum(kk * kk, axis=-1, keepdims=True)), 1e-12)
    k_dir = heads(k[:, :, None, :] * (1.0 + (a - 1.0) * lp['rwkv_k_a']))
    decay, a = heads(decay), heads(a)
    r, v = heads(r), heads(v)
    ln_g = lp['rwkv_ln_g'].reshape(A_HEADS, HEAD_DIM)
    ln_b = lp['rwkv_ln_b'].reshape(A_HEADS, HEAD_DIM)
    y_fwd = rwkv7_direction(r, decay[:, :, 0], k_dir[:, :, 0], v, kk, a[:, :, 0],
                            lp['rwkv_r_k'], ln_g, ln_b, False)
    y_bwd = rwkv7_direction(r, decay[:, :, 1], k_dir[:, :, 1], v, kk, a[:, :, 1],
                            lp['rwkv_r_k'], ln_g, ln_b, True)
    return (y_fwd + y_bwd).reshape(bsz, t_len, A_DIM) * g

def neighbourhood_attention(p, rpb):
    bsz, t_len, _ = p.shape
    rows = t_len // GRID_W
    kh = min(NA_KH_MAX, rows)
    q, k, v = jnp.split(p, 3, axis=-1)

    def grid(t):
        return t.reshape(bsz, rows, GRID_W, B_HEADS, HEAD_DIM)

    q = grid(q) * (HEAD_DIM ** -0.5)
    k, v = grid(k), grid(v)
    col = jnp.arange(GRID_W)
    col_start = jnp.clip(col - NA_KW // 2, 0, GRID_W - NA_KW)
    col_ok = (col[None, :] >= col_start[:, None]) & (col[None, :] < col_start[:, None] + NA_KW)
    dx_idx = jnp.clip(col[None, :] - col[:, None] + NA_KW - 1, 0, 2 * NA_KW - 2)

    def row_block(r):
        rs = jnp.clip(r - kh // 2, 0, rows - kh)
        kb = lax.dynamic_slice_in_dim(k, rs, kh, axis=1)
        vb = lax.dynamic_slice_in_dim(v, rs, kh, axis=1)
        qr = lax.dynamic_index_in_dim(q, r, axis=1, keepdims=False)
        dy_idx = rs + jnp.arange(kh) - r + NA_KH_MAX - 1
        bias = rpb[:, dy_idx[None, :, None], dx_idx[:, None, :]].astype(jnp.float32)
        s = jnp.einsum('bqhd,bkwhd->bhqkw', qr, kb).astype(jnp.float32) + bias
        s = jnp.where(col_ok[:, None, :], s, -jnp.inf)
        pr = jax.nn.softmax(s.reshape(bsz, B_HEADS, GRID_W, kh * GRID_W), axis=-1)
        pr = pr.reshape(s.shape).astype(vb.dtype)
        return jnp.einsum('bhqkw,bkwhd->bqhd', pr, vb)

    o = lax.map(row_block, jnp.arange(rows))
    return jnp.moveaxis(o, 0, 1).reshape(bsz, t_len, B_DIM)

def hyena_filters(seq_len, lp):
    f32 = jnp.float32
    t = jnp.linspace(0.0, 1.0, seq_len, dtype=f32)[:, None]
    w = 2.0 * math.pi * jnp.arange(seq_len, dtype=f32)[:, None] / seq_len
    f = jnp.linspace(1e-4, HY_BANDS - 1, HY_BANDS, dtype=f32)[None, :]
    z = jnp.concatenate([t, jnp.cos(f * w), -jnp.sin(f * w)], axis=-1)
    freq = lp['hy_sin_freq'].astype(f32)
    h = jnp.sin(freq * (z @ lp['hy_ff_w1'].astype(f32) + lp['hy_ff_b1'].astype(f32)))
    h = jnp.sin(freq * (h @ lp['hy_ff_w2'].astype(f32) + lp['hy_ff_b2'].astype(f32)))
    h = (h @ lp['hy_ff_w3'].astype(f32)).reshape(seq_len, 2, HY_ORDER, C_DIM)
    max_decay = math.log(HY_TARGET) / HY_FAST_DECAY_PCT
    min_decay = math.log(HY_TARGET) / HY_SLOW_DECAY_PCT
    deltas = jnp.linspace(min_decay, max_decay, C_DIM, dtype=f32)
    h = h * jnp.exp(-t * jnp.abs(deltas))[:, None, None, :]
    h_fwd, h_bwd = h[:, 0], h[:, 1]
    kern = jnp.concatenate([h_fwd, jnp.zeros((1, HY_ORDER, C_DIM), f32), jnp.flip(h_bwd[1:], axis=0)], axis=0)
    return kern / jnp.sum(jnp.abs(kern), axis=0, keepdims=True)

def fft_long_conv(u, kern_fft, seq_len):
    u_fft = jnp.fft.rfft(u, n=2 * seq_len, axis=1)
    return jnp.fft.irfft(u_fft * kern_fft[None], n=2 * seq_len, axis=1)[:, :seq_len]

def hyena_mixer(p, lp):
    seq_len = p.shape[1]
    cw = lp['hy_conv_w']
    p = shift_prev(p) * cw[0] + p * cw[1] + shift_next(p) * cw[2] + lp['hy_conv_b']
    v, x1, x2 = jnp.split(p.astype(jnp.float32), HY_ORDER + 1, axis=-1)
    kern_fft = jnp.fft.rfft(hyena_filters(seq_len, lp), axis=0)
    d_skip = lp['hy_bias'].astype(jnp.float32)
    z = x1 * (fft_long_conv(v, kern_fft[:, 0], seq_len) + v * d_skip[0])
    return x2 * (fft_long_conv(z, kern_fft[:, 1], seq_len) + z * d_skip[1])

def encoder_layer(x, lp):
    x = x + 0.5 * swiglu(rms_norm(x, lp['norm_ffn1']), lp['ffn1_w_in'], lp['ffn1_w_out'])
    h = rms_norm(x, lp['norm_mix'])
    proj = h @ lp['w_in']
    pa, pb, pc = jnp.split(proj, [A_COLS, A_COLS + B_COLS], axis=-1)
    ya = rwkv7_mixer(pa, lp)
    yb = group_rms_norm(neighbourhood_attention(pb, lp['na_rpb']), lp['na_out_norm'], B_HEADS)
    yc = group_rms_norm(hyena_mixer(pc, lp), lp['hy_out_norm'], C_GROUPS)
    mixed = jnp.concatenate([ya, yb, yc], axis=-1).astype(x.dtype)
    x = x + mixed @ lp['w_out']
    x = x + 0.5 * swiglu(rms_norm(x, lp['norm_ffn2']), lp['ffn2_w_in'], lp['ffn2_w_out'])
    return x

def encoder_trunk(x, params, final_norm):
    for layer in range(DEPTH):
        lp = {name: arr[layer] for name, arr in params.items()}
        x = encoder_layer(x, lp)
    return rms_norm(x, final_norm)

def setup_inputs(seed: int = 0) -> dict:
    key = jax.random.key(seed)
    ks = iter(jax.random.split(key, 40))
    f32 = jnp.float32
    L = DEPTH

    def normal(shape, scale):
        return jax.random.normal(next(ks), shape, f32) * scale

    def uniform(shape, lo, hi):
        return jax.random.uniform(next(ks), shape, f32, lo, hi)

    def gain(shape):
        return 1.0 + 0.05 * jax.random.normal(next(ks), shape, f32)

    return {
        'x_prompt': normal((BATCH, SEQ, D_MODEL), 1.0),
        'x_sample': normal((DEC_BATCH, DEC_SEQ, D_MODEL), 1.0),
        'norm_ffn1': gain((L, D_MODEL)),
        'ffn1_w_in': normal((L, D_MODEL, 2 * D_FF), D_MODEL ** -0.5),
        'ffn1_w_out': normal((L, D_FF, D_MODEL), D_FF ** -0.5),
        'norm_mix': gain((L, D_MODEL)),
        'w_in': normal((L, D_MODEL, N_PROJ), D_MODEL ** -0.5),
        'rwkv_mu': uniform((L, A_COLS), 0.0, 1.0),
        'rwkv_w0': uniform((L, 2, A_DIM), -5.0, -0.5),
        'rwkv_w_up': normal((L, 2, A_LORA_W, A_DIM), 0.5 * A_LORA_W ** -0.5),
        'rwkv_a0': normal((L, 2, A_DIM), 0.5),
        'rwkv_a_up': normal((L, 2, A_LORA_A, A_DIM), 0.5 * A_LORA_A ** -0.5),
        'rwkv_g_up': normal((L, A_LORA_G, A_DIM), A_LORA_G ** -0.5),
        'rwkv_k_k': 0.85 + normal((L, A_DIM), 0.05),
        'rwkv_k_a': 1.0 + normal((L, A_DIM), 0.05),
        'rwkv_r_k': normal((L, A_HEADS, HEAD_DIM), 0.1),
        'rwkv_ln_g': gain((L, A_DIM)),
        'rwkv_ln_b': normal((L, A_DIM), 0.02),
        'na_rpb': normal((L, B_HEADS, 2 * NA_KH_MAX - 1, 2 * NA_KW - 1), 0.1),
        'na_out_norm': gain((L, B_DIM)),
        'hy_conv_w': normal((L, 3, C_COLS), 3 ** -0.5),
        'hy_conv_b': normal((L, C_COLS), 0.02),
        'hy_ff_w1': normal((L, HY_EMB, HY_FF), HY_EMB ** -0.5),
        'hy_ff_b1': normal((L, HY_FF), 0.5),
        'hy_ff_w2': normal((L, HY_FF, HY_FF), HY_FF ** -0.5),
        'hy_ff_b2': normal((L, HY_FF), 0.5),
        'hy_ff_w3': normal((L, HY_FF, 2 * HY_ORDER * C_DIM), HY_FF ** -0.5),
        'hy_sin_freq': gain((L, HY_FF)),
        'hy_bias': normal((L, HY_ORDER, C_DIM), 0.1),
        'hy_out_norm': gain((L, C_DIM)),
        'w_out': normal((L, D_MIX, D_MODEL), D_MIX ** -0.5),
        'norm_ffn2': gain((L, D_MODEL)),
        'ffn2_w_in': normal((L, D_MODEL, 2 * D_FF), D_MODEL ** -0.5),
        'ffn2_w_out': normal((L, D_FF, D_MODEL), D_FF ** -0.5),
        'final_norm': gain((D_MODEL,)),
    }

def reference(x_prompt, x_sample, norm_ffn1, ffn1_w_in, ffn1_w_out, norm_mix, w_in,
              rwkv_mu, rwkv_w0, rwkv_w_up, rwkv_a0, rwkv_a_up, rwkv_g_up, rwkv_k_k, rwkv_k_a,
              rwkv_r_k, rwkv_ln_g, rwkv_ln_b, na_rpb, na_out_norm, hy_conv_w, hy_conv_b,
              hy_ff_w1, hy_ff_b1, hy_ff_w2, hy_ff_b2, hy_ff_w3, hy_sin_freq, hy_bias, hy_out_norm,
              w_out, norm_ffn2, ffn2_w_in, ffn2_w_out, final_norm):
    params = {
        'norm_ffn1': norm_ffn1, 'ffn1_w_in': ffn1_w_in, 'ffn1_w_out': ffn1_w_out,
        'norm_mix': norm_mix, 'w_in': w_in,
        'rwkv_mu': rwkv_mu, 'rwkv_w0': rwkv_w0, 'rwkv_w_up': rwkv_w_up, 'rwkv_a0': rwkv_a0,
        'rwkv_a_up': rwkv_a_up, 'rwkv_g_up': rwkv_g_up, 'rwkv_k_k': rwkv_k_k, 'rwkv_k_a': rwkv_k_a,
        'rwkv_r_k': rwkv_r_k, 'rwkv_ln_g': rwkv_ln_g, 'rwkv_ln_b': rwkv_ln_b,
        'na_rpb': na_rpb, 'na_out_norm': na_out_norm,
        'hy_conv_w': hy_conv_w, 'hy_conv_b': hy_conv_b, 'hy_ff_w1': hy_ff_w1, 'hy_ff_b1': hy_ff_b1,
        'hy_ff_w2': hy_ff_w2, 'hy_ff_b2': hy_ff_b2, 'hy_ff_w3': hy_ff_w3, 'hy_sin_freq': hy_sin_freq,
        'hy_bias': hy_bias, 'hy_out_norm': hy_out_norm,
        'w_out': w_out, 'norm_ffn2': norm_ffn2, 'ffn2_w_in': ffn2_w_in, 'ffn2_w_out': ffn2_w_out,
    }
    y_prompt = encoder_trunk(x_prompt, params, final_norm)
    y_sample = encoder_trunk(x_sample, params, final_norm)
    return (y_prompt, y_sample)


_drawn_inputs = setup_inputs


def setup_inputs(seed=0):
    import zlib

    import numpy as np

    out = dict(_drawn_inputs(seed))
    spreads = {}
    factors = {'rwkv_w_up': 4.124,
     'rwkv_k_k': 3.459,
     'rwkv_ln_g': 2.741,
     'rwkv_ln_b': 3.666,
     'hy_out_norm': 2.742,
     'norm_ffn2': 3.052}
    for name, (base, spread) in spreads.items():
        noise = np.random.default_rng([zlib.crc32(name.encode()), seed]).standard_normal(out[name].shape)
        drawn = base * np.exp(spread * noise) if base else spread * noise
        out[name] = jnp.asarray(drawn.astype(out[name].dtype))
    for name, factor in factors.items():
        out[name] = (out[name] * factor).astype(out[name].dtype)
    return out
```

```python
from contextlib import ExitStack

import numpy as np
import concourse.bass as bass
from concourse import mybir

F32 = mybir.dt.float32
ACT = mybir.ActivationFunctionType
ALU = mybir.AluOpType
AX = mybir.AxisListType

P = 128
LAYERS = 2
D = 1024
KT = D // P
SEQ, DEC = 512, 256
T = SEQ + DEC
SEGS = [(0, SEQ), (SEQ, DEC)]
HALF = T // 2
FF = 2816
FT = FF // P
HD = 64
GRID = 64
A_DIM, B_DIM, C_DIM = 256, 512, 256
A_TILES, C_TILES, QK_TILES, V_TILES = 8, 6, 8, 4
PROJ_TILES = A_TILES + C_TILES + QK_TILES + V_TILES
OUT_TILES = D // P
FF_USES = 2 * FT
USES = FF_USES + PROJ_TILES + OUT_TILES + FF_USES
CH = 64
CHUNKS = T // CH
HB = CHUNKS // 2
NORM_EPS, GN_EPS = 1e-5, 64e-5
DECAY_SCALE = -float(np.exp(-0.5))
TWO_PI_HI = 6.28125
TWO_PI_LO = float(2 * np.pi - 6.28125)
MAGIC = float(1.5 * 2 ** 23)
PI = 3.1415925
NEG = -1e30

PCOLS = [("norm_ffn1", 8), ("norm_mix", 8), ("norm_ffn2", 8), ("rwkv_mu", 8), ("rwkv_w0", 4), ("rwkv_a0", 4),
         ("rwkv_k_k", 2), ("rwkv_k_a", 2), ("rwkv_r_k", 2), ("rwkv_ln_g", 2), ("rwkv_ln_b", 2),
         ("na_out_norm", 4), ("hy_conv_w", 18), ("hy_conv_b", 6), ("hy_out_norm", 2),
         ("hy_ff_b1", 1), ("hy_ff_b2", 1), ("hy_sin_freq", 1), ("final_norm", 8)]
POFF = {}
NPAR = 0
for _name, _n in PCOLS:
    POFF[_name] = NPAR
    NPAR += _n
SCOLS = [("lora", 256), ("g_up", 256), ("rpb", 120)]
SOFF = {}
NSMALL = 0
for _name, _n in SCOLS:
    SOFF[_name] = NSMALL
    NSMALL += _n
CCOLS = [("ident", 128), ("ones", 128), ("blk", 128), ("masks", 512), ("eye", 64), ("alt", 1), ("wf", 6),
         ("shift", 128), ("colmask", 64)]
COFF = {}
NCONST = 0
for _name, _n in CCOLS:
    COFF[_name] = NCONST
    NCONST += _n
LOW_D, LOW_O, UP_D, UP_O, LOW_S, UP_S, LOW_I, UP_I = range(8)
HCOLS = [("cos", 2048), ("sin", 2048), ("decay", 1536), ("z", 768), ("altrow", 512)]
HWCOLS = [("w1", 64), ("w2", 64), ("w3", 1024), ("skip", 512)]
HWOFF = {"w1": 0, "w2": 64, "w3": 128, "skip": 1152}
NHW = 1664
HOFF = {}
NHY = 0
for _name, _n in HCOLS:
    HOFF[_name] = NHY
    NHY += _n


class Events:

    def __init__(self, sem, keys):
        self.sem, self.count, self.sent = sem, {k: i + 1 for i, k in enumerate(keys)}, 0
        assert len(self.count) == len(keys)

    def at(self, *key):
        return self.sem, self.count[key]

    def inc(self, *key):
        self.sent += 1
        assert self.count[key] == self.sent, (key, self.count[key], self.sent)
        return self.sem, 1


def build(nc, xT, wa, wb, par_d, small_d, const_d, hy_d, hw_d, outT):
    with ExitStack() as ctx:
        def sem(name):
            return ctx.enter_context(nc.semaphore(name))

        ctx.enter_context(nc.sbuf_tensor("fence", [P, 212000], mybir.dt.uint8))

        class Region:

            def __init__(self, at, end):
                self.at, self.end = (at + 31) // 32 * 32, end

            def __call__(self, name, shape):
                t = nc.alloc_sbuf_tensor_at(name, shape, F32, offset=self.at)
                self.at += (4 * int(np.prod(shape[1:])) + 31) // 32 * 32
                assert self.at <= self.end, (name, self.at, self.end)
                return t

        LIMIT = 229368
        fix = Region(16544, LIMIT)
        x = fix("x", [P, KT, T])
        h = fix("h", [P, KT, T])
        wring = fix("wring", [P, 4, KT, P])
        pool_at = fix.at
        fix("pool", [P, 15 * HALF])
        pool_end = fix.at
        rstd = fix("rstd", [P, T])
        par = fix("par", [P, NPAR])
        dpar = fix("dpar", [P, 20])
        eps = fix("eps", [P, 2])
        small = fix("small", [P, NSMALL])
        cst = fix("cst", [P, NCONST])
        arena = fix.at

        ra = Region(arena, LIMIT)
        act = ra("act", [P, FT, T])
        silu = ra("silu", [P, 2, HALF])
        rp_ = Region(pool_at, pool_end)
        wo_ring = [rp_(f"wo_ring{i}", [P, FT, P]) for i in range(2)]
        mixed = nc.alloc_sbuf_tensor_at("mixed", [P, OUT_TILES, T], F32, offset=arena)
        rw = Region(arena + 2 * 4 * T, LIMIT)
        kk = rw("kk", [P, 2, T])
        ksum = rw("ksum", [P, 2, T])
        vtok = rw("vtok", [P, 2, CHUNKS, CH])
        pa = rw("pa", [P, A_TILES, T])
        tmp_at = rw.at
        tmp = rw("tmp", [P, 4, T])
        rt = Region(tmp_at, rw.at)
        raw = [rt(f"raw{i}", [P, T + 3]) for i in range(2)]
        nbr = rt("nbr", [P, T + 1])
        ar = rw("ar", [P, CHUNKS, 2, CH])
        beta = rw("beta", [P, CHUNKS, CH])
        kap = rw("kap", [P, CHUNKS, CH])
        trans = rw("trans", [P, 2, CHUNKS, CH])
        inject = rw("inject", [P, 2, CHUNKS, CH])
        query = rw("query", [P, 2, CHUNKS, CH])
        olocal = rw("olocal", [P, 2, CHUNKS, CH])
        state = rw("state", [P, 2, CHUNKS, CH])
        scanm = rw("scanm", [P, T + 1])
        pc = rw("pc", [P, 2, CHUNKS])
        rb = Region(pool_at, pool_end)
        No, Lak, Mrb, Mrk, Na, Nb, Ma, Mb, X, btok, ktok = [
            rb(n, [P, HB, CH]) for n in ["No", "Lak", "Mrb", "Mrk", "Na", "Nb", "Ma", "Mb", "X", "btok", "ktok"]]
        R, Q = [rb(n, [P, HB, 2, CH]) for n in ["R", "Q"]]
        hy = Region(arena + OUT_TILES * 4 * T, LIMIT)
        hcos = hy("hcos", [P, 4, 512])
        hsin = hy("hsin", [P, 4, 512])
        ksin = hy("ksin", [P, 6, 512])
        altrow = hy("altrow", [1, 512])
        knyq = hy("knyq", [1, 2, 512])
        xnyq = hy("xnyq", [1, 2, 256])
        hy2 = Region(hy.at, LIMIT)
        se = hy("se", [P, 6, 512])
        so = hy("so", [P, 6, 512])
        hdecay = hy("hdecay", [P, 6, 256])
        hz = hy("hz", [P, T])
        h1 = hy("h1", [P, T])
        arg = hy("arg", [P, T])
        nrm = hy("nrm", [P, 2, 512])
        hwt = hy("hwt", [P, NHW])
        conv = hy2("conv", [P, C_TILES, T])
        vt, x1t, yc, ys, zt = [hy2(n, [P, 6, 256]) for n in ["vt", "x1t", "yc", "ys", "zt"]]
        hw = Region(pool_at, pool_end)
        kcos = hw("kcos", [P, 6, 512])
        hx = Region(hw.at, pool_end)
        prod = Region(hw.at, pool_end)("prod", [P, 4, 256])
        hraw = [hw(f"hraw{i}", [P, T + 3]) for i in range(2)]
        hnb = hw("hnb", [P, T + 1])
        hf, hb, af, ab, skipb = [hx(n, [P, 512]) for n in ["hf", "hb", "af", "ab", "skipb"]]
        na = Region(arena + OUT_TILES * 4 * T, LIMIT)
        qT = na("qT", [P, 4, T])
        kT = na("kT", [P, 4, T])
        vta = na("vta", [P, 6, 512])
        bias = na("bias", [P, 8, 16, 64])
        sc = na("sc", [P, 2, 512])
        nmax = na("nmax", [P, 2])
        ssum = na("ssum", [P, 2])
        rsum = na("rsum", [P, 2])
        nb = Region(pool_at, pool_end)
        pTp = [nb(f"pTp{i}", [P, 4, 512]) for i in range(2)]
        pTs = [nb(f"pTs{i}", [P, 2, 256]) for i in range(2)]

        ps = ctx.enter_context(nc.psum_tensor("ps", [P, 8, 512], F32))

        s_const, s_x, s_par = sem("const_loaded"), sem("x_loaded"), sem("par_loaded")
        s_hy = sem("hyena_tables_loaded")
        s_wa = [sem(f"w_tile_loaded{i}") for i in range(4)]
        s_wb = [sem(f"ffn_out_tile_loaded{i}") for i in range(2)]
        s_sq, s_sum, s_root, s_h = sem("norm_squares"), sem("norm_sums"), sem("norm_root"), sem("h_ready")
        s_gu, s_silu, s_act = sem("gate_up_ready"), sem("silu_done"), sem("act_done")
        s_fo, s_xup = sem("out_product_ready"), sem("x_updated")
        s_pj, s_raw, s_mixd = sem("proj_ready"), sem("raw_copied"), sem("raw_mixed")
        s_qk, s_qkc = sem("qkv_ready"), sem("qkv_copied")
        s_vstep, s_astep = sem("vector_step"), sem("scalar_step")
        s_bp, s_bv = sem("bias_products"), sem("bias_placed")
        s_sc, s_sm, s_pr, s_pn = sem("scores_ready"), sem("scores_biased"), sem("exp_done"), sem("probs_normed")
        s_tr, s_tc, s_pv, s_pvc = sem("probs_turned"), sem("turned_copied"), sem("attn_out"), sem("attn_out_copied")
        s_g1, s_g2, s_g3, s_g4 = sem("gnorm_squares"), sem("gnorm_sums"), sem("gnorm_root"), sem("gnorm_done")
        s_zero, s_eps, s_out = sem("pads_zeroed"), sem("eps_set"), sem("stored")

        L = range(LAYERS)
        DI = [(d, i) for d in range(2) for i in range(2)]
        BATCH = 10

        def layer_keys(fn):
            return [(l,) + k for l in L for k in fn()]

        def k_rp():
            out = []
            for i in range(2):
                out += [("ksq", i), ("vt", i)]
            for d in range(2):
                for i in range(2):
                    out += [("lora", d, i)] + [("b", d, i, f, s) for f in range(2) for s in range(BATCH)]
                out += [("chain", d, s) for s in range(2, 8)]
                for i in range(2):
                    out += [("read", d, i), ("mean", d, i), ("var", d, i)]
            return out + [("bonus", i) for i in range(2)]

        def k_ra():
            out = [("kroot", i) for i in range(2)] + [("tanh",)]
            for d in range(2):
                for i in range(2):
                    out += [("sig", d, i), ("expE", d, i), ("expL", d, i), ("expN", d, i)]
                    out += [("copy", d, i, f) for f in range(2)]
                for i in range(2):
                    out += [("osq", d, i), ("oroot", d, i)]
            return out

        def k_rv():
            out = []
            for i in range(2):
                out += [("ksq", i), ("vt", i), ("kk", i)]
            for d in range(2):
                for i in range(2):
                    out += [("cum", d, i), ("feat", d, i)]
                    out += [("b", d, i, f, s) for f in range(2) for s in range(BATCH)]
                out += [("state", d, s) for s in range(1, 8)]
                for i in range(2):
                    out += [("oread", d, i), ("ocen", d, i), ("onorm", d, i)]
            for i in range(2):
                out += [("rk", i), ("done", i)]
            return out

        def k_hp():
            out = [("f1",), ("f2",)]
            for p in range(6):
                out += [("f3", p), ("fabs", p)]
            out += [("kern", f) for f in range(6)] + [("tr", g) for g in range(6)]
            for o in range(2):
                out += [("dft", o, f) for f in range(6)]
                out += [("inv", o, t) for t in range(6 if o == 0 else 2)]
            return out

        def k_ha():
            return [("skip",), ("s1",), ("s2",)] + [("abs", p) for p in range(6)]

        def k_hv():
            out = [("a1",), ("a2",)]
            for p in range(6):
                out += [("win", p), ("eo", p)]
            out += [("norm",)] + [("kern", f) for f in range(6)] + [("tr", g) for g in range(6)]
            for o in range(2):
                out += [("dft", o, f) for f in range(6)]
                out += [("inv", o, t) for t in range(6 if o == 0 else 2)]
            return out

        rp, ra_, rv = (Events(sem(n), layer_keys(k)) for n, k in
                       (("rwkv_products", k_rp), ("rwkv_activated", k_ra), ("rwkv_vector", k_rv)))
        hp, ha, hv = (Events(sem(n), layer_keys(k)) for n, k in
                      (("hyena_products", k_hp), ("hyena_activated", k_ha), ("hyena_vector", k_hv)))

        def prm(name, i=0, rows=P):
            c = POFF[name] + i
            return par[0:rows, c:c + 1]

        def cs(name, p0=0, p1=P):
            return cst[p0:p1, COFF[name]:COFF[name] + dict(CCOLS)[name]]

        def mask(m):
            o = COFF["masks"] + CH * m
            return cst[:, o:o + CH].unsqueeze(1).broadcast_to([P, HB, CH])

        def eye_b(n=HB):
            return cs("eye").unsqueeze(1).broadcast_to([P, n, CH])

        def bank(b, n=512):
            return ps[:, b, 0:n]

        def units(b):
            return ps[:, b, 0:HALF].rearrange("p (c t) -> p c t", t=CH)

        def wide_units(b):
            return ps[:, b:b + 2, 0:HALF].rearrange("p b (c a t) -> p b c a t", a=2, t=CH)

        def mask3(m):
            o = COFF["masks"] + CH * m
            return cst[:, o:o + CH].unsqueeze(1).unsqueeze(1).broadcast_to([P, 2, HB // 2, CH])

        def split3(t):
            return t[:, :, :].rearrange("p (b c) t -> p b c t", b=2)

        def half_cols(t, i, f):
            return t[:, i, f * HB:(f + 1) * HB, :]

        def table(tab, kt, ft):
            if ft < 4:
                return tab[:, kt, P * ft:P * ft + P]
            return tab[:, kt, 256 * (ft - 4):256 * (ft - 4) + 256:2]

        def chain(d, s):
            out = [(s if d == 0 else 7 - s, 0)]
            if s < 4:
                out.append((8 + s if d == 0 else 11 - s, 1))
            return out

        def x_count(l, part):
            return 48 * l + {0: 0, 2: 16, 1: 32}[part]

        def use_base(l, part):
            return USES * l + [0, FF_USES, FF_USES + PROJ_TILES, FF_USES + PROJ_TILES + OUT_TILES][part]

        def tile_used(n):
            l, u = n // USES, n % USES
            if u < FF_USES:
                return s_gu, 2 * l * 2 * FT + 2 * (u // 2) + 2
            u -= FF_USES
            if u < A_TILES + C_TILES:
                return s_pj, 2 * (14 * l + u) + 2
            if u < A_TILES + C_TILES + QK_TILES:
                return s_qk, 14 * l + u - 14 + 1
            if u < PROJ_TILES:
                return s_qk, 14 * (l + 1)
            u -= PROJ_TILES
            if u < OUT_TILES:
                return s_fo, 48 * l + 16 + 2 * u + 2
            u -= OUT_TILES
            return s_gu, (2 * l + 1) * 2 * FT + 2 * (u // 2) + 2

        block = ctx.enter_context(nc.Block())

        @block.sync
        def _(sp):
            sp.dma_start(x[:, :, :], xT).then_inc(s_x, 16)
            sp.dma_start(cst[:, :], const_d).then_inc(s_const, 16)

            def load_tile(n):
                if n >= 4:
                    sp.wait_ge(*tile_used(n - 4))
                sp.dma_start(wring[:, n % 4, :, :],
                             wa[n // USES, n % USES].rearrange("p (k m) -> p k m", k=KT)).then_inc(s_wa[n % 4], 16)

            def load_out(l, f, m):
                n = (2 * l + f) * OUT_TILES + m
                if m < 2:
                    if n:
                        sp.wait_ge(s_xup, x_count(l, 1) if f else x_count(l, 0))
                else:
                    sp.wait_ge(s_fo, x_count(l, f) + 2 * (m - 1))
                sp.dma_start(wo_ring[n % 2][:, :, :],
                             wb[l, f, m].rearrange("p (k m) -> p k m", k=FT)).then_inc(s_wb[n % 2], 16)

            def load_ffn(l, f):
                for u in range(FF_USES):
                    load_tile(use_base(l, 3 if f else 0) + u)
                    if u in (8, 12):
                        load_out(l, f, (u - 8) // 4)
                for m in range(2, OUT_TILES):
                    load_out(l, f, m)

            for l in L:
                if l:
                    sp.wait_ge(s_h, 3 * l)
                sp.dma_start(par[:, :], par_d[l]).then_inc(s_par, 16)
                sp.dma_start(small[:, :], small_d[l]).then_inc(s_par, 16)
                load_ffn(l, 0)
                for u in range(A_TILES + 4):
                    load_tile(use_base(l, 1) + u)
                sp.wait_ge(*rv.at(l, "done", 1))
                for t, n in ((hcos, "cos"), (hsin, "sin"), (hdecay, "decay"), (hz, "z")):
                    flat = t[:, :, :].rearrange("p a b -> p (a b)") if len(t.shape) == 3 else t[:, :]
                    sp.dma_start(flat, hy_d[:, HOFF[n]:HOFF[n] + dict(HCOLS)[n]]).then_inc(s_hy, 16)
                sp.dma_start(altrow[:, :], hy_d[0:1, HOFF["altrow"]:HOFF["altrow"] + 512]).then_inc(s_hy, 16)
                sp.dma_start(hwt[:, :], hw_d[l]).then_inc(s_hy, 16)
                for u in range(A_TILES + 4, PROJ_TILES + OUT_TILES):
                    load_tile(use_base(l, 1) + u)
                load_ffn(l, 1)
            sp.wait_ge(s_h, 3 * LAYERS + 1)
            sp.dma_start(outT, h[:, :, :]).then_inc(s_out, 16)
            sp.wait_ge(s_out, 16)

        @block.tensor
        def _(pe):
            norms = [0]
            gns = [0]

            def mm(out, lhsT, rhs, start=True, stop=True):
                return pe.matmul(out, lhsT, rhs, start=start, stop=stop)

            def norm():
                pe.wait_ge(s_sq, norms[0] + 1)
                for f in range(2):
                    for c in range(KT):
                        m = mm(bank(6 + f, HALF), cs("ones"), h[:, c, f * HALF:(f + 1) * HALF], c == 0, c == KT - 1)
                    m.then_inc(s_sum, 1)
                norms[0] += 1

            def tile_in(n):
                pe.wait_ge(s_wa[n % 4], 16 * (n // 4 + 1))
                return wring[:, n % 4, :, :]

            def ffn(l, f):
                n0 = use_base(l, 3 if f else 0)
                u0 = (2 * l + f) * 2 * FT
                pe.wait_ge(s_h, norms[0])
                for j in range(FT):
                    w = tile_in(n0 + 2 * j), tile_in(n0 + 2 * j + 1)
                    for hf_ in range(2):
                        unit = u0 + 2 * j + hf_
                        if unit >= 2:
                            pe.wait_ge(s_act, unit - 1)
                        for side in range(2):
                            for c in range(KT):
                                m = mm(bank(2 * (unit % 2) + side, HALF), w[side][:, c, :],
                                       h[:, c, hf_ * HALF:(hf_ + 1) * HALF], c == 0, c == KT - 1)
                        m.then_inc(s_gu, 1)
                pe.wait_ge(s_act, u0 + 2 * FT)
                for m_ in range(OUT_TILES):
                    n = (2 * l + f) * OUT_TILES + m_
                    pe.wait_ge(s_wb[n % 2], 16 * (n // 2 + 1))
                    for hf_ in range(2):
                        v = 2 * m_ + hf_
                        if v >= 4:
                            pe.wait_ge(s_xup, x_count(l, f) + v - 3)
                        for k in range(FT):
                            m = mm(bank(4 + v % 4, HALF), wo_ring[n % 2][:, k, :], act[:, k, hf_ * HALF:(hf_ + 1) * HALF],
                                   k == 0, k == FT - 1)
                        m.then_inc(s_fo, 1)

            def proj(l, i):
                w = tile_in(use_base(l, 1) + i)
                pi = 14 * l + i
                if pi >= 2:
                    pe.wait_ge(s_raw, 2 * (pi - 1))
                for s, (t0, tn) in enumerate(SEGS):
                    for c in range(KT):
                        m = mm(bank(2 * (pi % 2) + s, tn), w[:, c, :], h[:, c, t0:t0 + tn], c == 0, c == KT - 1)
                    m.then_inc(s_pj, 1)

            def both(b, lhs, rhs, start=True, stop=True):
                for c in range(HB):
                    for hd in range(2):
                        r = slice(64 * hd, 64 * hd + 64)
                        m = mm(ps[r, b, CH * c:CH * c + CH], lhs(r, c), rhs(r, c), start, stop)
                return m

            def pair(b, lhs, rhs, lhs2, rhs2):
                for c in range(HB):
                    for hd in range(2):
                        r = slice(64 * hd, 64 * hd + 64)
                        o = ps[r, b, CH * c:CH * c + CH]
                        mm(o, lhs(r, c), rhs(r, c), True, False)
                        m = mm(o, lhs2(r, c), rhs2(r, c), False, True)
                return m

            def wide(b, lhs, rhs):
                for c in range(HB):
                    for hd in range(2):
                        r = slice(64 * hd, 64 * hd + 64)
                        m = mm(ps[r, b + c // 3, P * (c % 3):P * (c % 3) + P], lhs(r, c),
                               rhs(r, c).rearrange("p a t -> p (a t)"))
                return m

            def batch(l, d, i, f):
                c0 = f * HB
                al = lambda r, c: ar[r, c0 + c, 0, :]
                arr = lambda r, c: ar[r, c0 + c, :, :]
                be = lambda r, c: beta[r, c0 + c, :]
                ka = lambda r, c: kap[r, c0 + c, :]
                vv = lambda r, c: vtok[r, i, c0 + c, :]
                ey = lambda r, c: cs("eye")[r, :]
                B = lambda t: (lambda r, c: t[r, c, :])
                W = lambda t, a: (lambda r, c: t[r, c, a, :])
                WW = lambda t: (lambda r, c: t[r, c, :, :])
                k = (l, "b", d, i, f)
                both(0, al, be)
                wide(1, be, arr)
                wide(3, ka, arr)
                both(5, be, ey)
                both(6, ka, ey)
                both(7, al, ey).then_inc(*rp.inc(*k, 0))
                pe.wait_ge(*rv.at(*k, 0))
                both(0, B(Lak), vv)
                both(1, B(Ma), B(Na))
                both(2, B(Na), B(Ma)).then_inc(*rp.inc(*k, 1))
                pe.wait_ge(*rv.at(*k, 1))
                both(3, B(Nb), B(X))
                both(4, B(Mb), B(Nb))
                both(5, B(Nb), B(Mb)).then_inc(*rp.inc(*k, 2))
                pe.wait_ge(*rv.at(*k, 2))
                both(0, B(Na), B(X))
                both(1, B(Ma), B(Na)).then_inc(*rp.inc(*k, 3))
                pe.wait_ge(*rv.at(*k, 3))
                both(2, B(Nb), B(X)).then_inc(*rp.inc(*k, 4))
                pe.wait_ge(*rv.at(*k, 4))
                both(3, B(No), B(X))
                both(4, B(X), B(No))
                wide(5, B(X), WW(R)).then_inc(*rp.inc(*k, 5))
                pe.wait_ge(*rv.at(*k, 5))
                both(7, B(Na), B(Ma)).then_inc(*rp.inc(*k, 6))
                pe.wait_ge(*rv.at(*k, 6))
                wide(0, B(Mb), WW(Q)).then_inc(*rp.inc(*k, 7))
                pe.wait_ge(*rv.at(*k, 7))
                wide(2, B(Ma), WW(R)).then_inc(*rp.inc(*k, 8))
                pe.wait_ge(*rv.at(*k, 8))
                both(4, W(Q, 0), B(btok))
                pair(5, B(btok), W(Q, 1), B(ktok), vv)
                both(6, W(Q, 0), B(Mrb))
                pair(7, W(Q, 1), B(Mrb), vv, B(Mrk)).then_inc(*rp.inc(*k, 9))

            def rwkv(l):
                blk = cs("blk")
                for i in range(2):
                    pe.wait_ge(*rv.at(l, "ksq", i))
                    for s, (t0, tn) in enumerate(SEGS):
                        m = mm(bank(s, tn), blk, tmp[:, 1, t0:t0 + tn])
                    m.then_inc(*rp.inc(l, "ksq", i))
                    for f in range(2):
                        for c in range(HB):
                            for hd in range(2):
                                r = slice(64 * hd, 64 * hd + 64)
                                t0 = (f * HB + c) * CH
                                m = mm(ps[r, 2 + f, CH * c:CH * c + CH], pa[r, 4 + i, t0:t0 + CH], cs("eye")[r, :])
                    m.then_inc(*rp.inc(l, "vt", i))
                    pe.wait_ge(*rv.at(l, "kk", i))
                pe.wait_ge(*ra_.at(l, "tanh"))
                for d in range(2):
                    for i in range(2):
                        for s, (t0, tn) in enumerate(SEGS):
                            wr, arow = slice(32 * d, 32 * d + 32), slice(64 + 32 * d, 96 + 32 * d)
                            lo = SOFF["lora"] + P * i
                            mm(bank(s, tn), small[wr, lo:lo + P], pa[wr, 6, t0:t0 + tn])
                            m = mm(bank(2 + s, tn), small[arow, lo:lo + P], pa[arow, 6, t0:t0 + tn])
                        m.then_inc(*rp.inc(l, "lora", d, i))
                        pe.wait_ge(*rv.at(l, "feat", d, i))
                        for f in range(2):
                            batch(l, d, i, f)
                            pe.wait_ge(*rv.at(l, "b", d, i, f, 9))
                    for s in range(2, 8):
                        pe.wait_ge(*rv.at(l, "state", d, s - 1))
                        for i in range(2):
                            for c, col in chain(d, s - 1):
                                for hd in range(2):
                                    r = slice(64 * hd, 64 * hd + 64)
                                    m = mm(ps[r, 0, (2 * i + col) * CH:(2 * i + col + 1) * CH], trans[r, i, c, :],
                                           state[r, i, c, :])
                        m.then_inc(*rp.inc(l, "chain", d, s))
                    pe.wait_ge(*rv.at(l, "state", d, 7))
                    for i in range(2):
                        for f in range(2):
                            c0 = f * HB
                            m = both(f, lambda r, c: state[r, i, c0 + c, :], lambda r, c: query[r, i, c0 + c, :])
                        m.then_inc(*rp.inc(l, "read", d, i))
                        pe.wait_ge(*rv.at(l, "oread", d, i))
                        for f in range(2):
                            m = mm(units(2 + f), blk, half_cols(olocal, i, f))
                        m.then_inc(*rp.inc(l, "mean", d, i))
                        pe.wait_ge(*ra_.at(l, "osq", d, i))
                        for f in range(2):
                            m = mm(bank(4 + f, HALF), blk, tmp[:, 0, f * HALF:(f + 1) * HALF])
                        m.then_inc(*rp.inc(l, "var", d, i))
                for i in range(2):
                    pe.wait_ge(*rv.at(l, "rk", i))
                    for s, (t0, tn) in enumerate(SEGS):
                        mm(bank(s, tn), blk, tmp[:, 0, t0:t0 + tn])
                        lo = SOFF["g_up"] + P * i
                        m = mm(bank(2 + s, tn), small[0:64, lo:lo + P], pa[0:64, 7, t0:t0 + tn])
                    m.then_inc(*rp.inc(l, "bonus", i))

            def gnorm():
                pe.wait_ge(s_g1, gns[0] + 1)
                for f in range(2):
                    m = mm(bank(6 + f, HALF), cs("blk"), rstd[:, f * HALF:(f + 1) * HALF])
                m.then_inc(s_g2, 1)
                gns[0] += 1

            def filters(l):
                pe.wait_ge(s_hy, 16 * 6 * (l + 1))
                for s, (t0, tn) in enumerate(SEGS):
                    mm(ps[0:64, s, 0:tn], hwt[0:33, 0:64], hz[0:33, t0:t0 + tn])
                mm(bank(2), cs("ones", 0, 1), hwt[0:1, HWOFF["skip"]:HWOFF["skip"] + 512]).then_inc(*hp.inc(l, "f1"))
                pe.wait_ge(*ha.at(l, "s1"))
                for s, (t0, tn) in enumerate(SEGS):
                    m = mm(ps[0:64, s, 0:tn], hwt[0:64, 64:128], h1[0:64, t0:t0 + tn])
                m.then_inc(*hp.inc(l, "f2"))
                pe.wait_ge(*ha.at(l, "s2"))
                for p in range(6):
                    if p:
                        pe.wait_ge(*hv.at(l, "win", p - 1))
                    for dr in range(2):
                        lo = HWOFF["w3"] + 512 * dr
                        m = mm(bank(dr), h1[0:64, P * p:P * p + P], hwt[0:64, lo:lo + 512])
                    m.then_inc(*hp.inc(l, "f3", p))
                    pe.wait_ge(*ha.at(l, "abs", p))
                    s, k = (0, p) if p < 4 else (1, p - 4)
                    mm(bank(6 + s), cs("ones"), af[:, :], k == 0, False)
                    mm(bank(6 + s), cs("ones"), ab[:, :], False, k == (3 if s == 0 else 1)).then_inc(*hp.inc(l, "fabs", p))
                pe.wait_ge(*hv.at(l, "eo", 5))
                for ft in range(6):
                    if ft:
                        pe.wait_ge(*hv.at(l, "kern", ft - 1))
                    s, kts = (0, 4) if ft < 4 else (1, 2)
                    for kt in range(kts):
                        mm(bank(0), table(hcos, kt, ft), se[:, 4 * s + kt, :], kt == 0, kt == kts - 1)
                    for kt in range(kts):
                        m = mm(bank(1), table(hsin, kt, ft), so[:, 4 * s + kt, :], kt == 0, kt == kts - 1)
                    if ft in (0, 4):
                        for kt in range(kts):
                            m = mm(ps[0:1, 2, :], cs("alt"), se[:, 4 * s + kt, :], kt == 0, kt == kts - 1)
                    m.then_inc(*hp.inc(l, "kern", ft))

            def hyena(l):
                pe.wait_ge(s_mixd, 14 * (l + 1))
                for g in range(6):
                    if g >= 2:
                        pe.wait_ge(*hv.at(l, "tr", g - 2))
                    for j in range(4):
                        m = pe.transpose(ps[:, 4 + g % 2, P * j:P * j + P], conv[:, j, P * g:P * g + P], cs("ident"))
                    m.then_inc(*hp.inc(l, "tr", g))
                for o in range(2):
                    if o == 0:
                        pe.wait_ge(*hv.at(l, "tr", 5))
                    src = vt if o == 0 else zt
                    for ft in range(6):
                        if ft >= 1:
                            pe.wait_ge(*hv.at(l, "dft", o, ft - 1))
                        s, kts = (0, 4) if ft < 4 else (1, 2)
                        for half, tab in ((0, hcos), (1, hsin)):
                            for kt in range(kts):
                                m = mm(ps[:, ft % 2, 256 * half:256 * half + 256], table(tab, kt, ft), src[:, 4 * s + kt, :],
                                       kt == 0, kt == kts - 1)
                        if ft in (0, 4):
                            for kt in range(kts):
                                m = mm(ps[0:1, 2, 0:256], cs("alt"), src[:, 4 * s + kt, :], kt == 0, kt == kts - 1)
                        m.then_inc(*hp.inc(l, "dft", o, ft))
                    pe.wait_ge(*hv.at(l, "dft", o, 5))
                    if o == 0:
                        for tt in range(6):
                            if tt >= 2:
                                pe.wait_ge(*hv.at(l, "inv", 0, tt - 2))
                            s, kts = (0, 4) if tt < 4 else (1, 2)
                            out = ps[:, 4 + tt % 2, 0:256]
                            for kt in range(kts):
                                mm(out, table(hcos, kt, tt), yc[:, 4 * s + kt, :], kt == 0, False)
                                mm(out, table(hsin, kt, tt), ys[:, 4 * s + kt, :], False, False)
                            mm(out, altrow[0:1, 0:P], xnyq[0:1, s, :], False, True).then_inc(*hp.inc(l, "inv", 0, tt))
                        pe.wait_ge(*hv.at(l, "inv", 0, 5))
                    else:
                        for i in range(2):
                            if i:
                                pe.wait_ge(*hv.at(l, "inv", 1, 0))
                            for s, (t0, tn) in enumerate(SEGS):
                                kts = 4 if s == 0 else 2
                                out = bank(4 + s, tn)
                                for kt in range(kts):
                                    for tab, y in ((hcos, yc), (hsin, ys)):
                                        rhs = tab[:, kt, :] if s == 0 else tab[:, kt, 0:512:2]
                                        mm(out, y[:, 4 * s + kt, P * i:P * i + P], rhs, kt == 0 and tab is hcos, False)
                                m = mm(out, xnyq[0:1, s, P * i:P * i + P], altrow[0:1, 0:tn], False, True)
                            m.then_inc(*hp.inc(l, "inv", 1, i))
                for i in range(2):
                    gnorm()

            def attention(l):
                for g in range(16):
                    if 16 * l + g >= 2:
                        pe.wait_ge(s_bv, 16 * l + g - 1)
                    for k in range(4):
                        lo = COFF["shift"] + 63 - (4 * g + k)
                        for half in range(2):
                            m = mm(ps[64 * half:64 * half + 64, 4 + g % 2, 120 * k:120 * k + 120], cst[0:31, lo:lo + 64],
                                   small[0:31, SOFF["rpb"]:SOFF["rpb"] + 120])
                    m.then_inc(s_bp, 1)
                for i in range(QK_TILES):
                    w = tile_in(use_base(l, 1) + A_TILES + C_TILES + i)
                    if i >= 2:
                        pe.wait_ge(s_qkc, 14 * l + i - 1)
                    for s, (t0, tn) in enumerate(SEGS):
                        for c in range(KT):
                            m = mm(bank(2 * (i % 2) + s, tn), w[:, c, :], h[:, c, t0:t0 + tn], c == 0, c == KT - 1)
                    m.then_inc(s_qk, 1)
                pe.wait_ge(s_bv, 16 * (l + 1))
                pe.wait_ge(s_qkc, 14 * l + 8)
                ws = [tile_in(use_base(l, 1) + A_TILES + C_TILES + QK_TILES + i) for i in range(4)]
                for tt in range(6):
                    if tt >= 2:
                        pe.wait_ge(s_qkc, 14 * l + 8 + tt - 1)
                    for j in range(4):
                        for c in range(KT):
                            m = mm(ps[:, tt % 2, P * j:P * j + P], h[:, c, P * tt:P * tt + P], ws[j][:, c, :],
                                   c == 0, c == KT - 1)
                    m.then_inc(s_qk, 1)
                pe.wait_ge(s_qkc, 14 * (l + 1))

                def scores(u):
                    hd, i = u // 6, u % 6
                    r = slice(64 * (hd % 2), 64 * (hd % 2) + 64)
                    k0, kn = (0, 512) if i < 4 else (512, 256)
                    n = 48 * l + u
                    if n >= 2:
                        pe.wait_ge(s_sm, n - 1)
                    mm(bank(u % 2, kn), qT[r, hd // 2, P * i:P * i + P], kT[r, hd // 2, k0:k0 + kn]).then_inc(s_sc, 1)

                def turn(u):
                    n = 48 * l + u
                    pe.wait_ge(s_pn, n + 1)
                    if n >= 2:
                        pe.wait_ge(s_tc, n - 1)
                    for k in range(4 if u % 6 < 4 else 2):
                        m = pe.transpose(ps[:, 2 + u % 2, P * k:P * k + P], sc[:, u % 2, P * k:P * k + P], cs("ident"))
                    m.then_inc(s_tr, 1)

                def weigh(hd):
                    r = slice(64 * (hd % 2), 64 * (hd % 2) + 64)
                    pe.wait_ge(s_tc, 48 * l + 6 * hd + 6)
                    if hd >= 1:
                        pe.wait_ge(s_pvc, 8 * l + hd)
                    for k in range(4):
                        mm(ps[r, 4, :], vta[:, k, HD * hd:HD * hd + HD], pTp[hd % 2][:, k, :], k == 0, k == 3)
                    for k in range(2):
                        m = mm(ps[r, 5, 0:256], vta[:, 4 + k, HD * hd:HD * hd + HD], pTs[hd % 2][:, k, :], k == 0, k == 1)
                    m.then_inc(s_pv, 1)

                for u in range(49):
                    if u < 48:
                        scores(u)
                    if u:
                        turn(u - 1)
                        if u % 6 == 0:
                            weigh(u // 6 - 1)
                for i in range(4):
                    gnorm()

            def mix_out(l):
                pe.wait_ge(s_g4, 6 * (l + 1))
                for m_ in range(OUT_TILES):
                    w = tile_in(use_base(l, 2) + m_)
                    for f in range(2):
                        v = 2 * m_ + f
                        if v >= 4:
                            pe.wait_ge(s_xup, x_count(l, 2) + v - 3)
                        for k in range(OUT_TILES):
                            m = mm(bank(v % 4, HALF), w[:, k, :], mixed[:, k, f * HALF:(f + 1) * HALF], k == 0, k == 7)
                        m.then_inc(s_fo, 1)

            pe.wait_ge(s_const, 16)
            for l in L:
                pe.wait_ge(s_par, 32 * (l + 1))
                norm()
                ffn(l, 0)
                norm()
                pe.wait_ge(s_h, norms[0])
                for i in range(A_TILES):
                    proj(l, i)
                rwkv(l)
                filters(l)
                pe.wait_ge(*hv.at(l, "kern", 5))
                for i in range(C_TILES):
                    proj(l, A_TILES + i)
                hyena(l)
                attention(l)
                mix_out(l)
                norm()
                ffn(l, 1)
            norm()

        @block.scalar
        def _(sa):
            A = sa.activation
            norms = [0]
            gns = [0]

            def norm():
                for f in range(2):
                    sa.wait_ge(s_sum, 2 * norms[0] + f + 1)
                    A(rstd[:, f * HALF:(f + 1) * HALF], bank(6 + f, HALF), ACT.Sqrt,
                      bias=eps[:, 0:1], scale=1.0 / D).then_inc(s_root, 1)
                norms[0] += 1

            def ffn(l, f):
                for u in range((2 * l + f) * 2 * FT, (2 * l + f + 1) * 2 * FT):
                    sa.wait_ge(s_gu, u + 1)
                    if u >= 2:
                        sa.wait_ge(s_act, u - 1)
                    A(silu[:, u % 2, :], bank(2 * (u % 2), HALF), ACT.Silu).then_inc(s_silu, 1)

            def copy_raw(l, i, bufs):
                pi = 14 * l + i
                for s, (t0, tn) in enumerate(SEGS):
                    sa.wait_ge(s_pj, 2 * pi + s + 1)
                    if pi >= 2 and s == 0:
                        sa.wait_ge(s_mixd, pi - 1)
                    sa.copy(bufs[pi % 2][:, 1 + t0 + s:1 + t0 + s + tn], bank(2 * (pi % 2) + s, tn)).then_inc(s_raw, 1)

            def rwkv(l):
                for i in range(2):
                    sa.wait_ge(*rp.at(l, "ksq", i))
                    for s, (t0, tn) in enumerate(SEGS):
                        m = A(tmp[:, 2, t0:t0 + tn], bank(s, tn), ACT.Sqrt, scale=float(HD))
                    m.then_inc(*ra_.inc(l, "kroot", i))
                A(pa[0:64, 7, :], pa[0:64, 7, :], ACT.Sigmoid)
                A(pa[0:64, 6, :], pa[0:64, 6, :], ACT.Tanh).then_inc(*ra_.inc(l, "tanh"))
                for d in range(2):
                    for i in range(2):
                        sa.wait_ge(*rp.at(l, "lora", d, i))
                        if (d, i) != (0, 0):
                            dd, ii = DI[DI.index((d, i)) - 1]
                            sa.wait_ge(*rv.at(l, "feat", dd, ii))
                        if d == 1 and i == 0:
                            sa.wait_ge(*rv.at(l, "onorm", 0, 1))
                        for s, (t0, tn) in enumerate(SEGS):
                            A(tmp[:, 0, t0:t0 + tn], bank(s, tn), ACT.Sigmoid, bias=prm("rwkv_w0", 2 * d + i))
                            m = A(tmp[:, 1, t0:t0 + tn], bank(2 + s, tn), ACT.Sigmoid, bias=prm("rwkv_a0", 2 * d + i))
                        m.then_inc(*ra_.inc(l, "sig", d, i))
                        sa.wait_ge(*rv.at(l, "cum", d, i))
                        A(tmp[:, 0, :], tmp[:, 0, :], ACT.Exp).then_inc(*ra_.inc(l, "expE", d, i))
                        A(tmp[:, 3, :], tmp[:, 2, :], ACT.Exp).then_inc(*ra_.inc(l, "expL", d, i))
                        A(tmp[:, 2, :], tmp[:, 2, :], ACT.Exp, scale=-1.0).then_inc(*ra_.inc(l, "expN", d, i))
                        for f in range(2):
                            sa.wait_ge(*rp.at(l, "b", d, i, f, 0))
                            sa.copy(btok[:, :, :], units(5))
                            sa.copy(ktok[:, :, :], units(6)).then_inc(*ra_.inc(l, "copy", d, i, f))
                    for i in range(2):
                        sa.wait_ge(*rv.at(l, "ocen", d, i))
                        A(tmp[:, 0, :], olocal[:, i, :, :].rearrange("p c t -> p (c t)"), ACT.Square)\
                            .then_inc(*ra_.inc(l, "osq", d, i))
                        sa.wait_ge(*rp.at(l, "var", d, i))
                        for f in range(2):
                            m = A(tmp[:, 1, f * HALF:(f + 1) * HALF], bank(4 + f, HALF), ACT.Sqrt, bias=eps[:, 1:2])
                        m.then_inc(*ra_.inc(l, "oroot", d, i))

            def gn(tile):
                if gns[0]:
                    sa.wait_ge(s_g4, gns[0])
                A(rstd[:, :], mixed[:, tile, :], ACT.Square).then_inc(s_g1, 1)
                sa.wait_ge(s_g2, gns[0] + 1)
                for f in range(2):
                    m = A(rstd[:, f * HALF:(f + 1) * HALF], bank(6 + f, HALF), ACT.Sqrt, bias=eps[:, 0:1])
                m.then_inc(s_g3, 1)
                gns[0] += 1

            def filters(l):
                sa.wait_ge(*hp.at(l, "f1"))
                sa.copy(skipb[:, :], bank(2)).then_inc(*ha.inc(l, "skip"))
                for n in (1, 2):
                    sa.wait_ge(*hv.at(l, f"a{n}"))
                    A(h1[0:64, :], arg[0:64, :], ACT.Sin).then_inc(*ha.inc(l, f"s{n}"))
                for p in range(6):
                    sa.wait_ge(*hv.at(l, "win", p))
                    if p:
                        sa.wait_ge(*hp.at(l, "fabs", p - 1))
                    A(af[:, :], hf[:, :], ACT.Abs)
                    A(ab[:, :], hb[:, :], ACT.Abs).then_inc(*ha.inc(l, "abs", p))

            def attention(l):
                for i in range(QK_TILES):
                    sa.wait_ge(s_qk, 14 * l + i + 1)
                    dst = qT if i < 4 else kT
                    for s, (t0, tn) in enumerate(SEGS):
                        m = sa.copy(dst[:, i % 4, t0:t0 + tn], bank(2 * (i % 2) + s, tn))
                    m.then_inc(s_qkc, 1)
                for tt in range(6):
                    sa.wait_ge(s_qk, 14 * l + 8 + tt + 1)
                    sa.copy(vta[:, tt, :], bank(tt % 2)).then_inc(s_qkc, 1)

                def exps(u):
                    kn = 512 if u % 6 < 4 else 256
                    sa.wait_ge(s_sm, 48 * l + u + 1)
                    A(sc[:, u % 2, 0:kn], sc[:, u % 2, 0:kn], ACT.Exp, bias=nmax[:, u % 2:u % 2 + 1],
                      accum_out=ssum[:, u % 2:u % 2 + 1]).then_inc(s_pr, 1)

                def turned(u):
                    hd, i = u // 6, u % 6
                    sa.wait_ge(s_tr, 48 * l + u + 1)
                    if i == 0 and 8 * l + hd >= 2:
                        sa.wait_ge(s_pv, 8 * l + hd - 1)
                    if i < 4:
                        dst, kn = pTp[hd % 2][:, :, P * i:P * i + P], 4
                    else:
                        dst, kn = pTs[hd % 2][:, :, P * (i - 4):P * (i - 3)], 2
                    sa.copy(dst, ps[:, 2 + u % 2, 0:P * kn].rearrange("p (k q) -> p k q", q=P)).then_inc(s_tc, 1)
                    if i == 5:
                        r = slice(64 * (hd % 2), 64 * (hd % 2) + 64)
                        sa.wait_ge(s_pv, 8 * l + hd + 1)
                        sa.copy(mixed[r, 2 + hd // 2, 0:512], ps[r, 4, :])
                        sa.copy(mixed[r, 2 + hd // 2, 512:768], ps[r, 5, 0:256]).then_inc(s_pvc, 1)

                for u in range(49):
                    if u < 48:
                        exps(u)
                    if u:
                        turned(u - 1)

            sa.wait_ge(s_eps, 1)
            for l in L:
                sa.wait_ge(s_par, 32 * (l + 1))
                norm()
                ffn(l, 0)
                norm()
                sa.wait_ge(s_zero, 2 * l + 1)
                for i in range(A_TILES):
                    copy_raw(l, i, raw)
                sa.wait_ge(s_mixd, 14 * l + A_TILES)
                rwkv(l)
                filters(l)
                sa.wait_ge(s_zero, 2 * l + 2)
                for i in range(A_TILES, A_TILES + C_TILES):
                    copy_raw(l, i, hraw)
                for i in range(2):
                    sa.wait_ge(*hv.at(l, "inv", 1, i))
                    gn(6 + i)
                attention(l)
                sa.wait_ge(s_pvc, 8 * (l + 1))
                for i in range(4):
                    gn(2 + i)
                sa.wait_ge(s_g4, 6 * (l + 1))
                norm()
                ffn(l, 1)
            norm()

        @block.vector
        def _(ve):
            norms = [0]
            gns = [0]
            steps = [0]
            TT, TS, STT = ve.tensor_tensor, ve.tensor_scalar, ve.scalar_tensor_tensor
            M, AD, SU = ALU.mult, ALU.add, ALU.subtract

            def step(ins):
                steps[0] += 1
                ins.then_inc(s_vstep, 1)
                ve.wait_ge(s_vstep, steps[0])

            def norm(gain, x_ready):
                ve.wait_ge(s_xup, x_ready)
                for c in range(KT):
                    m = TT(h[:, c, :], x[:, c, :], x[:, c, :], M)
                m.then_inc(s_sq, 1)
                ve.wait_ge(s_root, 2 * norms[0] + 2)
                step(ve.reciprocal(rstd[:, :], rstd[:, :]))
                for c in range(KT):
                    m = STT(h[:, c, :], x[:, c, :], prm(gain, c), rstd[:, :], M, M)
                m.then_inc(s_h, 1)
                norms[0] += 1

            def derive():
                mu, ka = POFF["rwkv_mu"], POFF["rwkv_k_a"]
                TS(dpar[:, 0:8], par[:, mu:mu + 8], -1.0, 1.0, M, AD)
                TS(dpar[:, 8:16], par[:, mu:mu + 8], 0.5, None, M)
                TS(dpar[:, 16:18], par[:, ka:ka + 2], -1.0, 1.0, M, AD)
                b1 = POFF["hy_ff_b1"]
                step(TS(dpar[:, 18:20], par[:, b1:b1 + 2], prm("hy_sin_freq"), None, M))

            def add_out(l, part, factor, banks):
                for v in range(16):
                    ve.wait_ge(s_fo, x_count(l, part) + v + 1)
                    xs = x[:, v // 2, (v % 2) * HALF:(v % 2 + 1) * HALF]
                    STT(xs, bank(banks + v % 4, HALF), factor, xs, M, AD).then_inc(s_xup, 1)

            def ffn(l, f):
                for v in range(2 * FT):
                    u = (2 * l + f) * 2 * FT + v
                    ve.wait_ge(s_silu, u + 1)
                    TT(act[:, v // 2, (v % 2) * HALF:(v % 2 + 1) * HALF], silu[:, u % 2, :],
                       bank(2 * (u % 2) + 1, HALF), M).then_inc(s_act, 1)
                add_out(l, f, 0.5, 4)

            def zero_pads(bufs):
                for b in bufs:
                    for c in (0, SEQ + 1, T + 2):
                        m = ve.memset(b[:, c:c + 1], 0.0)
                m.then_inc(s_zero, 1)

            def shift_mix(l, i):
                pi = 14 * l + i
                b = raw[pi % 2]
                ve.wait_ge(s_raw, 2 * pi + 2)
                step(TT(nbr[:, :], b[:, 0:T + 1], b[:, 2:T + 3], AD))
                step(TS(nbr[:, :], nbr[:, :], dpar[:, 8 + i:9 + i], None, M))
                for s, (t0, tn) in enumerate(SEGS):
                    m = STT(pa[:, i, t0:t0 + tn], b[:, 1 + t0 + s:1 + t0 + s + tn], dpar[:, i:i + 1],
                            nbr[:, t0 + s:t0 + s + tn], M, AD)
                m.then_inc(s_mixd, 1)
                ve.wait_ge(s_mixd, pi + 1)

            def conv_mix(l, i):
                pi = 14 * l + A_TILES + i
                b = hraw[pi % 2]
                ve.wait_ge(s_raw, 2 * pi + 2)
                step(TS(hnb[:, :], b[:, 1:T + 2], prm("hy_conv_w", 6 + i), prm("hy_conv_b", i), M, AD))
                step(STT(hnb[:, :], b[:, 0:T + 1], prm("hy_conv_w", i), hnb[:, :], M, AD))
                for s, (t0, tn) in enumerate(SEGS):
                    m = STT(conv[:, i, t0:t0 + tn], b[:, 2 + t0 + s:2 + t0 + s + tn], prm("hy_conv_w", 12 + i),
                            hnb[:, t0 + s:t0 + s + tn], M, AD)
                m.then_inc(s_mixd, 1)
                ve.wait_ge(s_mixd, pi + 1)

            def flat(t):
                return t.rearrange("p c t -> p (c t)")

            def batch(l, d, i, f):
                k = (l, "b", d, i, f)
                low, up = ((LOW_D, LOW_O, LOW_S, LOW_I), (UP_D, UP_O, UP_S, UP_I))[::1 if d == 0 else -1]
                ve.wait_ge(*rp.at(*k, 0))
                TT(Na[:, :, :], units(0), mask(low[0]), M)
                TT(No[:, :, :], units(0), mask(low[1]), M)
                w1, w3 = wide_units(1), wide_units(3)
                TT(split3(Ma), w1[:, :, :, 0, :], mask3(up[0]), M)
                TT(split3(Mrb), w1[:, :, :, 1, :], mask3(up[3]), M)
                TT(split3(Lak), w3[:, :, :, 0, :], mask3(up[2]), M)
                TT(split3(Mrk), w3[:, :, :, 1, :], mask3(up[3]), M)
                ve.wait_ge(*ra_.at(l, "copy", d, i, f))
                TS(R[:, :, 0, :], units(7), -1.0, None, M).then_inc(*rv.inc(*k, 0))
                ve.wait_ge(*rv.at(*k, 0))
                TT(X[:, :, :], Ma[:, :, :], eye_b(), AD)
                ve.wait_ge(*rp.at(*k, 1))
                TS(R[:, :, 1, :], units(0), -1.0, None, M)
                ve.tensor_copy(Nb[:, :, :], units(1))
                ve.tensor_copy(Mb[:, :, :], units(2)).then_inc(*rv.inc(*k, 1))
                ve.wait_ge(*rp.at(*k, 2))
                ve.wait_ge(*rv.at(*k, 1))
                TT(X[:, :, :], X[:, :, :], units(3), AD)
                ve.tensor_copy(Na[:, :, :], units(4))
                ve.tensor_copy(Ma[:, :, :], units(5)).then_inc(*rv.inc(*k, 2))
                ve.wait_ge(*rp.at(*k, 3))
                ve.wait_ge(*rv.at(*k, 2))
                TT(X[:, :, :], X[:, :, :], units(0), AD)
                ve.tensor_copy(Nb[:, :, :], units(1)).then_inc(*rv.inc(*k, 3))
                ve.wait_ge(*rp.at(*k, 4))
                ve.wait_ge(*rv.at(*k, 3))
                TT(X[:, :, :], X[:, :, :], units(2), AD).then_inc(*rv.inc(*k, 4))
                ve.wait_ge(*rp.at(*k, 5))
                ve.tensor_copy(Ma[:, :, :], units(3))
                ve.tensor_copy(Na[:, :, :], units(4))
                for b in range(2):
                    m = ve.tensor_copy(Q[:, 3 * b:3 * b + 3, :, :].rearrange("p c a t -> p (c a t)"), bank(5 + b, HALF))
                m.then_inc(*rv.inc(*k, 5))
                ve.wait_ge(*rp.at(*k, 6))
                ve.tensor_copy(Mb[:, :, :], units(7)).then_inc(*rv.inc(*k, 6))
                ve.wait_ge(*rp.at(*k, 7))
                ve.wait_ge(*rv.at(*k, 6))
                for b in range(2):
                    m = TT(R[:, 3 * b:3 * b + 3, :, :].rearrange("p c a t -> p (c a t)"),
                           Q[:, 3 * b:3 * b + 3, :, :].rearrange("p c a t -> p (c a t)"), bank(b, HALF), AD)
                m.then_inc(*rv.inc(*k, 7))
                ve.wait_ge(*rp.at(*k, 8))
                ve.wait_ge(*rv.at(*k, 7))
                for b in range(2):
                    m = TT(Q[:, 3 * b:3 * b + 3, :, :].rearrange("p c a t -> p (c a t)"),
                           R[:, 3 * b:3 * b + 3, :, :].rearrange("p c a t -> p (c a t)"), bank(2 + b, HALF), AD)
                m.then_inc(*rv.inc(*k, 8))
                ve.wait_ge(*rp.at(*k, 9))
                TT(half_cols(trans, i, f), units(4), eye_b(), AD)
                decay_end = pc[:, i, f * HB:(f + 1) * HB].unsqueeze(2).broadcast_to([P, HB, CH])
                TT(half_cols(inject, i, f), units(5), decay_end, M)
                TT(half_cols(query, i, f), units(6), ar[:, f * HB:(f + 1) * HB, 1, :], AD)
                ve.tensor_copy(half_cols(olocal, i, f), units(7)).then_inc(*rv.inc(*k, 9))

            def rwkv(l):
                c2 = lambda t, n: t[:, n, :]
                step(ve.memset(scanm[:, :], 1.0))
                m = ve.memset(scanm[:, 0:T + 1:CH], 0.0)
                step(m)
                for i in range(2):
                    step(TS(tmp[:, 0, :], pa[:, 2 + i, :], prm("rwkv_k_k", i), None, M))
                    TT(tmp[:, 1, :], tmp[:, 0, :], tmp[:, 0, :], M).then_inc(*rv.inc(l, "ksq", i))
                    ve.wait_ge(*rp.at(l, "vt", i))
                    for f in range(2):
                        m = ve.tensor_copy(half_cols(vtok, i, f), units(2 + f))
                    m.then_inc(*rv.inc(l, "vt", i))
                    ve.wait_ge(*ra_.at(l, "kroot", i))
                    step(TS(tmp[:, 2, :], tmp[:, 2, :], 1e-12, None, ALU.max))
                    step(ve.reciprocal(tmp[:, 2, :], tmp[:, 2, :]))
                    TT(kk[:, i, :], tmp[:, 0, :], tmp[:, 2, :], M).then_inc(*rv.inc(l, "kk", i))
                    ve.wait_ge(*rv.at(l, "kk", i))
                for d in range(2):
                    for i in range(2):
                        ve.wait_ge(*ra_.at(l, "sig", d, i))
                        step(TS(tmp[:, 0, :], tmp[:, 0, :], DECAY_SCALE, None, M))
                        if d == 0:
                            step(ve.tensor_tensor_scan(tmp[:, 2, :], scanm[:, 0:T], tmp[:, 0, :], 0.0, M, AD))
                        else:
                            step(ve.tensor_tensor_scan(tmp[:, 2, ::-1], scanm[:, T:0:-1], tmp[:, 0, ::-1], 0.0, M, AD))
                        TT(tmp[:, 0, :], tmp[:, 2, :], tmp[:, 0, :], SU).then_inc(*rv.inc(l, "cum", d, i))
                        step(TS(kap[:, :, :].rearrange("p c t -> p (c t)"), tmp[:, 1, :], prm("rwkv_k_a", i),
                                dpar[:, 16 + i:17 + i], M, AD))
                        kf, bf, k_in = flat(kap[:, :, :]), flat(beta[:, :, :]), pa[:, 2 + i, :]
                        step(TT(kf, kf, k_in, M))
                        if d == 0:
                            ve.tensor_copy(ksum[:, i, :], kf)
                        else:
                            TT(ksum[:, i, :], ksum[:, i, :], kf, AD)
                        step(TT(bf, kk[:, i, :], tmp[:, 1, :], M))
                        v3 = lambda t: t.rearrange("p (c t) -> p c t", t=CH)
                        ve.wait_ge(*ra_.at(l, "expE", d, i))
                        TT(ar[:, :, 0, :], v3(kk[:, i, :]), v3(tmp[:, 0, :]), M)
                        ve.wait_ge(*ra_.at(l, "expL", d, i))
                        TT(ar[:, :, 1, :], v3(pa[:, i, :]), v3(tmp[:, 3, :]), M)
                        ve.tensor_copy(pc[:, i, :], v3(tmp[:, 3, :])[:, :, CH - 1 if d == 0 else 0])
                        ve.wait_ge(*ra_.at(l, "expN", d, i))
                        TT(bf, bf, tmp[:, 2, :], M)
                        TT(kf, kf, tmp[:, 2, :], M).then_inc(*rv.inc(l, "feat", d, i))
                        ve.wait_ge(*rv.at(l, "feat", d, i))
                        for f in range(2):
                            batch(l, d, i, f)
                    ve.wait_ge(*rv.at(l, "b", d, 1, 1, 9))
                    for s in range(1, 8):
                        if s == 1:
                            for c, col in chain(d, 0):
                                ve.memset(state[:, :, c, :], 0.0)
                        else:
                            ve.wait_ge(*rp.at(l, "chain", d, s))
                        prev = chain(d, s - 1)
                        for c, col in chain(d, s):
                            pcol = [p for p, q in prev if q == col][0]
                            if s == 1:
                                m = ve.tensor_copy(state[:, :, c, :], inject[:, :, pcol, :])
                            else:
                                got = ps[:, 0, 0:256].rearrange("p (i q t) -> p i q t", i=2, q=2)[:, :, col, :]
                                de = pc[:, :, pcol].unsqueeze(2).broadcast_to([P, 2, CH])
                                step(TT(state[:, :, c, :], got, de, M))
                                m = TT(state[:, :, c, :], state[:, :, c, :], inject[:, :, pcol, :], AD)
                        m.then_inc(*rv.inc(l, "state", d, s))
                    for i in range(2):
                        ve.wait_ge(*rp.at(l, "read", d, i))
                        for f in range(2):
                            m = TT(half_cols(olocal, i, f), half_cols(olocal, i, f), units(f), AD)
                        m.then_inc(*rv.inc(l, "oread", d, i))
                        ve.wait_ge(*rp.at(l, "mean", d, i))
                        ve.wait_ge(*rv.at(l, "oread", d, i))
                        for f in range(2):
                            m = TT(half_cols(olocal, i, f), half_cols(olocal, i, f), units(2 + f), SU)
                        m.then_inc(*rv.inc(l, "ocen", d, i))
                        ve.wait_ge(*ra_.at(l, "oroot", d, i))
                        step(ve.reciprocal(tmp[:, 1, :], tmp[:, 1, :]))
                        o = flat(olocal[:, i, :, :])
                        step(TT(o, o, tmp[:, 1, :], M))
                        if d == 0:
                            m = TS(mixed[:, i, :], o, prm("rwkv_ln_g", i), prm("rwkv_ln_b", i), M, AD)
                        else:
                            step(TS(o, o, prm("rwkv_ln_g", i), prm("rwkv_ln_b", i), M, AD))
                            m = TT(mixed[:, i, :], mixed[:, i, :], o, AD)
                        m.then_inc(*rv.inc(l, "onorm", d, i))
                for i in range(2):
                    ve.wait_ge(*rv.at(l, "onorm", 1, 1))
                    TT_in = STT(tmp[:, 0, :], pa[:, i, :], prm("rwkv_r_k", i), ksum[:, i, :], M, M)
                    TT_in.then_inc(*rv.inc(l, "rk", i))
                    ve.wait_ge(*rp.at(l, "bonus", i))
                    for s, (t0, tn) in enumerate(SEGS):
                        step(STT(tmp[:, 1, t0:t0 + tn], bank(s, tn), float(HD), pa[:, 4 + i, t0:t0 + tn], M, M))
                    step(TT(mixed[:, i, :], mixed[:, i, :], tmp[:, 1, :], AD))
                    for s, (t0, tn) in enumerate(SEGS):
                        m = TT(mixed[:, i, t0:t0 + tn], mixed[:, i, t0:t0 + tn], bank(2 + s, tn), M)
                    m.then_inc(*rv.inc(l, "done", i))

            def gn(tile, gain, c):
                ve.wait_ge(s_g3, gns[0] + 1)
                step(ve.reciprocal(rstd[:, :], rstd[:, :]))
                STT(mixed[:, tile, :], mixed[:, tile, :], prm(gain, c), rstd[:, :], M, M).then_inc(s_g4, 1)
                gns[0] += 1

            def reduce_arg(l, n, column):
                ve.wait_ge(*hp.at(l, f"f{n}"))
                for s, (t0, tn) in enumerate(SEGS):
                    m = TS(arg[0:64, t0:t0 + tn], ps[0:64, s, 0:tn], prm("hy_sin_freq", 0, 64), dpar[0:64, column:column + 1], M, AD)
                step(m)
                a, r = arg[0:64, :], h1[0:64, :]
                step(TS(r, a, float(1 / (2 * np.pi)), MAGIC, M, AD))
                step(TS(r, r, -MAGIC, None, AD))
                step(STT(a, r, -TWO_PI_HI, a, M, AD))
                step(STT(a, r, -TWO_PI_LO, a, M, AD))
                TS(a, a, PI, -PI, ALU.min, ALU.max).then_inc(*hv.inc(l, f"a{n}"))

            def filters(l):
                reduce_arg(l, 1, 18)
                reduce_arg(l, 2, 19)
                for p in range(6):
                    ve.wait_ge(*hp.at(l, "f3", p))
                    if p:
                        ve.wait_ge(*hv.at(l, "eo", p - 1))
                    win = hdecay[:, p, :].unsqueeze(1).broadcast_to([P, 2, 256])
                    o2 = lambda t: t.rearrange("p (o c) -> p o c", o=2)
                    TT(o2(hf[:, :]), o2(bank(0)), win, M)
                    m = TT(o2(hb[:, :]), o2(bank(1)), win, M)
                    if p in (0, 4):
                        step(m)
                        m = ve.memset(hb[0:1, :], 0.0)
                    m.then_inc(*hv.inc(l, "win", p))
                    ve.wait_ge(*hv.at(l, "win", p))
                    TT(se[:, p, :], hf[:, :], hb[:, :], AD)
                    m = TT(so[:, p, :], hf[:, :], hb[:, :], SU)
                    m.then_inc(*hv.inc(l, "eo", p))
                    ve.wait_ge(*ha.at(l, "abs", p))
                ve.wait_ge(*hp.at(l, "fabs", 5))
                for s in range(2):
                    m = ve.reciprocal(nrm[:, s, :], bank(6 + s))
                m.then_inc(*hv.inc(l, "norm"))
                ve.wait_ge(*hv.at(l, "norm"))
                ve.wait_ge(*ha.at(l, "skip"))
                for ft in range(6):
                    s = 0 if ft < 4 else 1
                    wf = cst[:, COFF["wf"] + ft:COFF["wf"] + ft + 1]
                    ve.wait_ge(*hp.at(l, "kern", ft))
                    TT(kcos[:, ft, :], bank(0), nrm[:, s, :], M)
                    m = TT(ksin[:, ft, :], bank(1), nrm[:, s, :], M)
                    if ft in (0, 4):
                        m = TT(knyq[0:1, s, :], ps[0:1, 2, :], nrm[0:1, s, :], M)
                    step(m)
                    TS(ksin[:, ft, :], ksin[:, ft, :], wf, None, M)
                    m = TT(kcos[:, ft, :], kcos[:, ft, :], skipb[:, :], AD)
                    if ft in (0, 4):
                        m = TT(knyq[0:1, s, :], knyq[0:1, s, :], skipb[0:1, :], AD)
                    step(m)
                    m = TS(kcos[:, ft, :], kcos[:, ft, :], wf, None, M)
                    if ft in (0, 4):
                        m = TS(knyq[0:1, s, :], knyq[0:1, s, :], 0.5 / (SEQ, DEC)[s], None, M)
                    m.then_inc(*hv.inc(l, "kern", ft))

            def hyena(l):
                for g in range(6):
                    ve.wait_ge(*hp.at(l, "tr", g))
                    ve.tensor_copy(vt[:, g, :], ps[:, 4 + g % 2, 0:256])
                    ve.tensor_copy(x1t[:, g, :], ps[:, 4 + g % 2, 256:512]).then_inc(*hv.inc(l, "tr", g))
                for o in range(2):
                    kcol = slice(256 * o, 256 * o + 256)
                    for ft in range(6):
                        ve.wait_ge(*hp.at(l, "dft", o, ft))
                        xc, xs = ps[:, ft % 2, 0:256], ps[:, ft % 2, 256:512]
                        TT(prod[:, 0, :], xc, kcos[:, ft, kcol], M)
                        TT(prod[:, 1, :], xs, ksin[:, ft, kcol], M)
                        TT(prod[:, 2, :], xc, ksin[:, ft, kcol], M)
                        m = TT(prod[:, 3, :], xs, kcos[:, ft, kcol], M)
                        if ft in (0, 4):
                            s = ft // 4
                            m = TT(xnyq[0:1, s, :], ps[0:1, 2, 0:256], knyq[0:1, s, kcol], M)
                        step(m)
                        TT(yc[:, ft, :], prod[:, 0, :], prod[:, 1, :], SU)
                        TT(ys[:, ft, :], prod[:, 2, :], prod[:, 3, :], AD).then_inc(*hv.inc(l, "dft", o, ft))
                    if o == 0:
                        for tt in range(6):
                            ve.wait_ge(*hp.at(l, "inv", 0, tt))
                            TT(zt[:, tt, :], x1t[:, tt, :], ps[:, 4 + tt % 2, 0:256], M).then_inc(*hv.inc(l, "inv", 0, tt))
                    else:
                        for i in range(2):
                            ve.wait_ge(*hp.at(l, "inv", 1, i))
                            for s, (t0, tn) in enumerate(SEGS):
                                m = TT(mixed[:, 6 + i, t0:t0 + tn], conv[:, 4 + i, t0:t0 + tn], bank(4 + s, tn), M)
                            m.then_inc(*hv.inc(l, "inv", 1, i))
                for i in range(2):
                    gn(6 + i, "hy_out_norm", i)

            def attention(l):
                for g in range(16):
                    ve.wait_ge(s_bp, 16 * l + g + 1)
                    src = ps[:, 4 + g % 2, 0:480].rearrange("p (k h d) -> p h d k", k=4, h=8)
                    cm = COFF["colmask"] + 4 * g
                    for half in range(2):
                        r = slice(64 * half, 64 * half + 64)
                        for hd in range(8):
                            m = TT(bias[r, hd, half:half + 15, 4 * g:4 * g + 4], src[r, hd, :, :],
                                   cst[r, cm:cm + 4].unsqueeze(1).broadcast_to([64, 15, 4]), AD)
                    m.then_inc(s_bv, 1)

                def smooth(u):
                    hd, i = u // 6, u % 6
                    kn, rows, top = (512, 8, 7 - 2 * i) if i < 4 else (256, 4, 7 - 2 * (i - 4))
                    n = 48 * l + u
                    ve.wait_ge(s_sc, n + 1)
                    if n >= 2:
                        ve.wait_ge(s_tr, n - 1)
                    g = sc[:, u % 2, 0:kn]
                    step(STT(g.rearrange("p (r c) -> p r c", c=64), bank(u % 2, kn).rearrange("p (r c) -> p r c", c=64),
                             HD ** -0.5, bias[:, hd, top:top + rows, :], M, AD))
                    ve.tensor_reduce(nmax[:, u % 2:u % 2 + 1], g, AX.X, ALU.max, negate=True).then_inc(s_sm, 1)

                def normed(u):
                    kn = 512 if u % 6 < 4 else 256
                    ve.wait_ge(s_pr, 48 * l + u + 1)
                    step(ve.reciprocal(rsum[:, u % 2:u % 2 + 1], ssum[:, u % 2:u % 2 + 1]))
                    g = sc[:, u % 2, 0:kn]
                    TS(g, g, rsum[:, u % 2:u % 2 + 1], None, M).then_inc(s_pn, 1)

                ve.wait_ge(s_bv, 16 * (l + 1))
                for u in range(49):
                    if u < 48:
                        smooth(u)
                    if u:
                        normed(u - 1)
                for i in range(4):
                    gn(2 + i, "na_out_norm", i)

            ve.memset(eps[:, 0:1], NORM_EPS)
            ve.memset(eps[:, 1:2], GN_EPS).then_inc(s_eps, 1)
            ve.wait_ge(s_x, 16)
            ve.wait_ge(s_const, 16)
            for l in L:
                ve.wait_ge(s_par, 32 * (l + 1))
                derive()
                norm("norm_ffn1", x_count(l, 0))
                ffn(l, 0)
                norm("norm_mix", x_count(l, 2))
                zero_pads(raw)
                for i in range(A_TILES):
                    shift_mix(l, i)
                rwkv(l)
                ve.wait_ge(s_hy, 96 * (l + 1))
                filters(l)
                zero_pads(hraw)
                for i in range(C_TILES):
                    conv_mix(l, i)
                hyena(l)
                attention(l)
                add_out(l, 2, 1.0, 0)
                norm("norm_ffn2", x_count(l, 1))
                ffn(l, 1)
            norm("final_norm", x_count(LAYERS, 0))


def constants():
    c = np.zeros((P, NCONST), np.float32)
    p = np.arange(P)
    row, col = (p % CH)[:, None], np.arange(CH)[None, :]

    def put(name, v):
        c[0:v.shape[0], COFF[name]:COFF[name] + v.shape[1]] = v

    put("ident", np.eye(P))
    put("ones", np.ones((P, P)))
    put("blk", (p[:, None] // HD == p[None, :] // HD) / float(HD))
    low, up, same = col < row, col > row, col // 16 == row // 16
    put("masks", np.concatenate([-1.0 * (low & same), -1.0 * (low & ~same), -1.0 * (up & same), -1.0 * (up & ~same),
                                 1.0 * low, 1.0 * up, 1.0 * (col <= row), 1.0 * (col >= row)], 1))
    put("eye", 1.0 * (col == row))
    put("alt", (1.0 - 2.0 * (p % 2))[:, None])
    wf = np.zeros((P, 6))
    for ft in range(6):
        n = SEQ if ft < 4 else DEC
        wf[:, ft] = 1.0 / n
    wf[0, 0], wf[0, 4] = 0.5 / SEQ, 0.5 / DEC
    put("wf", wf)
    m = np.arange(P)
    put("shift", 1.0 * (np.arange(31)[:, None] == 78 - m[None, :]))
    qc, kc = (p % GRID)[:, None], np.arange(GRID)[None, :]
    start = np.clip(qc - 8, 0, GRID - 16)
    put("colmask", np.where((kc >= start) & (kc < start + 16), 0.0, NEG))
    return c


def hyena_constants():
    c = np.zeros((P, NHY), np.float32)
    n = np.arange(512)
    ang = 2 * np.pi * ((n[:, None] * n[None, :]) % 1024) / 1024.0
    rows = lambda a: a.reshape(4, P, 512).transpose(1, 0, 2).reshape(P, 2048)
    c[:, HOFF["cos"]:HOFF["cos"] + 2048] = rows(np.cos(ang))
    c[:, HOFF["sin"]:HOFF["sin"] + 2048] = rows(np.sin(ang))
    deltas = np.abs(np.linspace(np.log(1e-2) / 1.5, np.log(1e-2) / 0.3, C_DIM))
    for s, (t0, tn) in enumerate(SEGS):
        t = np.linspace(0.0, 1.0, tn)
        dec = np.exp(-t[:, None] * deltas[None, :]).reshape(tn // P, P, C_DIM).transpose(1, 0, 2)
        o = HOFF["decay"] + 256 * (t0 // P)
        c[:, o:o + 256 * (tn // P)] = dec.reshape(P, -1)
        w = 2 * np.pi * np.arange(tn) / tn
        f = np.linspace(1e-4, 15, 16)
        fw = f[:, None] * w[None, :]
        z = np.concatenate([t[None, :], np.cos(fw), -np.sin(fw)], 0)
        c[0:33, HOFF["z"] + t0:HOFF["z"] + t0 + tn] = z
    c[:, HOFF["altrow"]:HOFF["altrow"] + 512] = 1.0 - 2.0 * (n % 2)
    return c


def pack(inputs):
    a = {k: np.ascontiguousarray(v) for k, v in inputs.items()}
    x = np.concatenate([a["x_prompt"][0], a["x_sample"][0]], 0)
    out = {"xT": np.ascontiguousarray(x.T.reshape(KT, P, T).transpose(1, 0, 2))}

    def tiles(w):
        k, n = w.shape
        return w.reshape(k // P, P, n // P, P).transpose(2, 1, 0, 3).reshape(n // P, P, -1)

    wa, wb, par, small, hw = [], [], [], [], []
    for l in range(LAYERS):
        def ffn_in(w):
            t = tiles(w)
            return np.stack([t[:FT], t[FT:]], 1).reshape(FF_USES, P, -1)
        w = a["w_in"][l]
        gate_pad = np.concatenate([w[:, 896:960], np.zeros((D, 64), np.float32)], 1)
        wp = np.concatenate([w[:, 0:896], gate_pad, w[:, 960 + 1536:], w[:, 960:960 + 1536]], 1)
        wa.append(np.concatenate([ffn_in(a["ffn1_w_in"][l]), tiles(wp), tiles(a["w_out"][l]), ffn_in(a["ffn2_w_in"][l])], 0))
        wb.append(np.stack([tiles(a["ffn1_w_out"][l]), tiles(a["ffn2_w_out"][l])], 0))
        pr = np.zeros((P, NPAR), np.float32)
        for name, n in PCOLS:
            v = (a[name] if name == "final_norm" else a[name][l]).reshape(-1)
            if v.size < n * P:
                v = np.concatenate([v, np.zeros(n * P - v.size, np.float32)])
            pr[:, POFF[name]:POFF[name] + n] = v.reshape(n, P).T
        par.append(pr)
        sm = np.zeros((P, NSMALL), np.float32)
        sm[:, SOFF["lora"]:SOFF["lora"] + 256] = np.concatenate(
            [a["rwkv_w_up"][l].reshape(64, 256), a["rwkv_a_up"][l].reshape(64, 256)], 0)
        sm[0:64, SOFF["g_up"]:SOFF["g_up"] + 256] = a["rwkv_g_up"][l]
        sm[0:31, SOFF["rpb"]:SOFF["rpb"] + 120] = a["na_rpb"][l].transpose(2, 0, 1).reshape(31, 120)
        small.append(sm)
        hh = np.zeros((P, NHW), np.float32)
        hh[0:33, 0:64] = a["hy_ff_w1"][l]
        hh[0:64, 64:128] = a["hy_ff_w2"][l]
        hh[0:64, 128:1152] = a["hy_ff_w3"][l]
        hh[0:1, 1152:1664] = a["hy_bias"][l].reshape(1, 512)
        hw.append(hh)
    out.update(wa=np.stack(wa), wb=np.stack(wb), par=np.stack(par), small=np.stack(small),
               const=constants(), hyc=hyena_constants(), hyw=np.stack(hw))
    return out


def kernel(**inputs):
    import concourse.bacc as _bacc
    from concourse.bass_utils import run_bass_kernel_spmd as _run

    arrays = pack(inputs)
    nc = _bacc.Bacc("TRN2", target_bir_lowering=False, num_devices=1)
    args = [nc.dram_tensor(n, v.shape, mybir.dt.from_np(v.dtype), kind="ExternalInput").ap() for n, v in arrays.items()]
    args.append(nc.dram_tensor("outT", (P, KT, T), F32, kind="ExternalOutput").ap())
    build(nc, *args)
    r = _run(nc, [arrays], core_ids=[0])
    y = r.results[0]["outT"].transpose(2, 1, 0).reshape(T, D)
    return np.ascontiguousarray(y[:SEQ][None]), np.ascontiguousarray(y[SEQ:][None])
```

```python
from contextlib import ExitStack

import numpy as np
import concourse.bass as bass
from concourse import mybir

F32 = mybir.dt.float32
F32R = mybir.dt.float32r
BF16 = mybir.dt.bfloat16
ACT = mybir.ActivationFunctionType
ALU = mybir.AluOpType
AX = mybir.AxisListType

P = 128
LAYERS = 2
D = 1024
KT = D // P
SEQ, DEC = 512, 256
T = SEQ + DEC
SEGS = [(0, SEQ), (SEQ, DEC)]
HALF = T // 2
FF = 2816
FT = FF // P
HD = 64
GRID = 64
A_DIM, B_DIM, C_DIM = 256, 512, 256
A_TILES, C_TILES, QK_TILES, V_TILES = 8, 6, 8, 4
PROJ_TILES = A_TILES + C_TILES + QK_TILES + V_TILES
OUT_TILES = D // P
FF_BLOCKS = [(0, 8), (8, 8), (16, 6)]
FF_USES = 2 * FT + len(FF_BLOCKS) * OUT_TILES
RAWS, SPLITS = 3, 4
USES = FF_USES + PROJ_TILES + OUT_TILES + FF_USES
CH = 64
CHUNKS = T // CH
HB = CHUNKS // 2
NORM_EPS, GN_EPS = 1e-5, 64e-5
DECAY_SCALE = -float(np.exp(-0.5))
TWO_PI_HI = 6.28125
TWO_PI_LO = float(2 * np.pi - 6.28125)
MAGIC = float(1.5 * 2 ** 23)
PI = 3.1415925
NEG = -1e30

PCOLS = [("norm_ffn1", 8), ("norm_mix", 8), ("norm_ffn2", 8), ("rwkv_mu", 8), ("rwkv_w0", 4), ("rwkv_a0", 4),
         ("rwkv_k_k", 2), ("rwkv_k_a", 2), ("rwkv_r_k", 2), ("rwkv_ln_g", 2), ("rwkv_ln_b", 2),
         ("na_out_norm", 4), ("hy_conv_w", 18), ("hy_conv_b", 6), ("hy_out_norm", 2),
         ("hy_ff_b1", 1), ("hy_ff_b2", 1), ("hy_sin_freq", 1), ("final_norm", 8)]
POFF = {}
NPAR = 0
for _name, _n in PCOLS:
    POFF[_name] = NPAR
    NPAR += _n
SCOLS = [("lora", 256), ("g_up", 256), ("rpb", 120)]
SOFF = {}
NSMALL = 0
for _name, _n in SCOLS:
    SOFF[_name] = NSMALL
    NSMALL += _n
CCOLS = [("ident", 128), ("ones", 128), ("blk", 128), ("masks", 512), ("eye", 64), ("alt", 1), ("wf", 6),
         ("shift", 128), ("colmask", 64)]
COFF = {}
NCONST = 0
for _name, _n in CCOLS:
    COFF[_name] = NCONST
    NCONST += _n
LOW_D, LOW_O, UP_D, UP_O, LOW_S, UP_S, LOW_I, UP_I = range(8)
HCOLS = [("cos", 2048), ("sin", 2048), ("decay", 1536), ("z", 768), ("altrow", 512)]
HWCOLS = [("w1", 64), ("w2", 64), ("w3", 1024), ("skip", 512)]
HWOFF = {"w1": 0, "w2": 64, "w3": 128, "skip": 1152}
NHW = 1664
HOFF = {}
NHY = 0
for _name, _n in HCOLS:
    HOFF[_name] = NHY
    NHY += _n


class Events:

    def __init__(self, sem, keys):
        self.sem, self.count, self.sent = sem, {k: i + 1 for i, k in enumerate(keys)}, 0
        assert len(self.count) == len(keys)

    def at(self, *key):
        return self.sem, self.count[key]

    def inc(self, *key):
        self.sent += 1
        assert self.count[key] == self.sent, (key, self.count[key], self.sent)
        return self.sem, 1


def build(nc, xT, wa, par_d, small_d, const_d, hy_d, hw_d, outT):
    with ExitStack() as ctx:
        def sem(name):
            return ctx.enter_context(nc.semaphore(name))

        ctx.enter_context(nc.sbuf_tensor("fence", [P, 212000], mybir.dt.uint8))

        class Region:

            def __init__(self, at, end):
                self.at, self.end = (at + 31) // 32 * 32, end

            def __call__(self, name, shape, dtype=F32):
                t = nc.alloc_sbuf_tensor_at(name, shape, dtype, offset=self.at)
                self.at += (4 * int(np.prod(shape[1:])) + 31) // 32 * 32
                assert self.at <= self.end, (name, self.at, self.end)
                return t

        LIMIT = 229368
        TILE = 4 * T
        fix = Region(16544, LIMIT)
        x = fix("x", [P, KT, T])
        wring = fix("wring", [P, RAWS, KT, P])
        rstd = fix("rstd", [P, T])
        par = fix("par", [P, NPAR])
        dpar = fix("dpar", [P, 20])
        eps = fix("eps", [P, 3])
        small = fix("small", [P, NSMALL])
        cst = fix("cst", [P, NCONST])
        Z = fix.at
        Z_SPLIT = Z + 2 * KT * TILE
        Z_MIXED = Z_SPLIT + 2 * SPLITS * 4 * KT * P
        Z_AFTER = Z_MIXED + OUT_TILES * TILE

        hsp = Region(Z, Z_SPLIT)
        hh, hl = [hsp(n, [P, KT, T], F32R) for n in ["hh", "hl"]]
        wsp = Region(Z_SPLIT, Z_MIXED)
        wh, wl = [wsp(n, [P, SPLITS, KT, P], F32R) for n in ["wh", "wl"]]
        msp = Region(Z, Z_SPLIT)
        mh, ml = [msp(n, [P, OUT_TILES, T], F32R) for n in ["mh", "ml"]]
        hout = nc.alloc_sbuf_tensor_at("hout", [P, KT, T], F32, offset=Z)
        top = Region(LIMIT - 2 * TILE - 64, LIMIT)
        sqb = top("sqb", [P, 2, T])
        ra = Region(Z_MIXED, LIMIT - 2 * TILE - 64)
        ah, al_ = [ra(n, [P, 8, T], F32R) for n in ["act_high", "act_low"]]
        silu = ra("silu", [P, 2, HALF])
        gated = ra("gated", [P, 2, HALF])
        mixed = nc.alloc_sbuf_tensor_at("mixed", [P, OUT_TILES, T], F32, offset=Z_MIXED)
        rw = Region(Z_MIXED + 2 * TILE, LIMIT)
        kk = rw("kk", [P, 2, T])
        ksum = rw("ksum", [P, 2, T])
        vtok = rw("vtok", [P, 2, CHUNKS, CH])
        pa = rw("pa", [P, A_TILES, T])
        tmp_at = rw.at
        tmp = rw("tmp", [P, 4, T])
        rt = Region(tmp_at, rw.at)
        raw = [rt(f"raw{i}", [P, T + 3]) for i in range(2)]
        nbr = rt("nbr", [P, T + 1])
        ar = rw("ar", [P, CHUNKS, 2, CH])
        vbd = rw("values_bd", [P, CHUNKS, 2, CH])
        btok_bd = rw("btok_bd", [P, CHUNKS, 2, CH])
        Q1_ = rw("Q1", [P, HB, 2, CH])
        beta_bd = btok_bd
        xs = Region(16544, 16544 + KT * TILE)
        Na_bd, Ma_bd, No_bd, G_bd = [xs(n + "_bd", [P, CHUNKS, 2, CH]) for n in ["Na", "Ma", "No", "G"]]
        Lak_bd = Nb_bd = X_bd = G_bd
        Q0_bd = Na_bd
        rb = Region(Z, Z_MIXED)
        trans = rb("trans", [P, 2, CHUNKS, CH])
        inject = rb("inject", [P, 2, CHUNKS, CH])
        query = rb("query", [P, 2, CHUNKS, CH])
        olocal = rb("olocal", [P, 2, CHUNKS, CH])
        state = rb("state", [P, 2, CHUNKS, CH])
        pc = rb("pc", [P, 2, CHUNKS])
        rb.at = (rb.at + 31) // 32 * 32
        scanm = nc.alloc_sbuf_tensor_at("scanm", [P, T + 1], BF16, offset=rb.at)
        rb.at += 2 * T + 32
        ktok_bd = rb("ktok_bd", [P, CHUNKS, 2, CH])
        kap_bd = ktok_bd
        Mb_bd = rb("Mb_bd", [P, CHUNKS, 2, CH])
        alpha_bd = Q1_bd = Mb_bd
        Na, Ma, No, Mrk, Nb = [rb(n, [P, CHUNKS, CH]) for n in ["Na", "Ma", "No", "Mrk", "Nb"]]
        Mb_X = rb("Mb_X", [P, CHUNKS, 2, CH])
        btok_Mrb = rb("btok_Mrb", [P, CHUNKS, 2, CH])
        Mb, X = Mb_X[:, :, 0, :], Mb_X[:, :, 1, :]
        btok, Mrb = btok_Mrb[:, :, 0, :], btok_Mrb[:, :, 1, :]
        beta, kap = Nb, Na
        R = rb("R", [P, CHUNKS, 2, CH])
        Q = [rb("Q0", [P, HB, 2, CH]), Q1_]
        aft = Region(Z_AFTER, LIMIT)
        conv = aft("conv", [P, C_TILES, T])
        q_at = aft.at
        qT = aft("qT", [P, 4, T])
        kT = aft("kT", [P, 4, T])
        vta = aft("vta", [P, 6, 512])
        hw = Region(q_at, LIMIT)
        hraw = [hw(f"hraw{i}", [P, T + 3]) for i in range(2)]
        hnb = hw("hnb", [P, T + 1])
        na = Region(Z, Z_MIXED)
        bias = na("bias", [P, 8, 16, 64])
        SCB = 4
        sc = na("sc", [P, SCB, 512])
        nmax, ssum, rsum = [na(n, [P, SCB]) for n in ["nmax", "ssum", "rsum"]]
        pTp = [na(f"pTp{i}", [P, 4, 512]) for i in range(2)]
        pTs = [na(f"pTs{i}", [P, 2, 256]) for i in range(2)]
        hy = Region(Z, Z_MIXED)
        hcos = hy("hcos", [P, 4, 512])
        hsin = hy("hsin", [P, 4, 512])
        ksin = hy("ksin", [P, 6, 512])
        kcos = hy("kcos", [P, 6, 512])
        altrow = hy("altrow", [1, 512])
        knyq = hy("knyq", [1, 2, 512])
        xnyq = hy("xnyq", [1, 2, 256])
        hy1 = Region(hy.at, Z_MIXED)
        hdecay = hy1("hdecay", [P, 6, 256])
        hz = hy1("hz", [P, T])
        h1 = hy1("h1", [P, T])
        arg = hy1("arg", [P, T])
        nrm = hy1("nrm", [P, 2, 512])
        hwt = hy1("hwt", [P, NHW])
        hy2 = Region(q_at, LIMIT)
        se = hy2("se", [P, 6, 512])
        so = hy2("so", [P, 6, 512])
        hf, hb, af, ab, skipb = [hy2(n, [P, 512]) for n in ["hf", "hb", "af", "ab", "skipb"]]
        hy3 = Region(q_at, LIMIT)
        vt, x1t, yc, ys, zt = [hy3(n, [P, 6, 256]) for n in ["vt", "x1t", "yc", "ys", "zt"]]
        prod = hy3("prod", [P, 4, 256])

        LAG = 3
        ps = ctx.enter_context(nc.psum_tensor("ps", [P, 8, 512], F32))

        s_const, s_x, s_par = sem("const_loaded"), sem("x_loaded"), sem("par_loaded")
        s_hz, s_hy = sem("filter_inputs_loaded"), sem("hyena_tables_loaded")
        s_wa = [sem(f"w_tile_loaded{i}") for i in range(RAWS)]
        s_whi, s_w = sem("w_high_ready"), sem("w_split_ready")
        s_sq, s_acc, s_sum, s_root = sem("norm_squares"), sem("norm_squares_added"), sem("norm_sums"), sem("norm_root")
        s_ht, s_hhi, s_h = sem("h_tile_normed"), sem("h_high_ready"), sem("h_split_ready")
        s_gu, s_silu, s_mul, s_ahi, s_act = (sem(n) for n in (
            "gate_up_ready", "silu_done", "gated", "act_high_ready", "act_split_ready"))
        s_mhi, s_m, s_fin = sem("mixed_high_ready"), sem("mixed_split_ready"), sem("final_ready")
        s_fo, s_xup = sem("out_product_ready"), sem("x_updated")
        s_pj, s_raw, s_mixd = sem("proj_ready"), sem("raw_copied"), sem("raw_mixed")
        s_qk, s_qkc = sem("qkv_ready"), sem("qkv_copied")
        s_vstep, s_astep = sem("vector_step"), sem("scalar_step")
        s_bp, s_bv = sem("bias_products"), sem("bias_placed")
        s_sc, s_sm, s_pr, s_pn = sem("scores_ready"), sem("scores_biased"), sem("exp_done"), sem("probs_normed")
        s_tr, s_tc, s_pv, s_pvc = sem("probs_turned"), sem("turned_copied"), sem("attn_out"), sem("attn_out_copied")
        s_g1, s_g2, s_g3, s_g4 = sem("gnorm_squares"), sem("gnorm_sums"), sem("gnorm_root"), sem("gnorm_done")
        s_zero, s_eps, s_out = sem("pads_zeroed"), sem("eps_set"), sem("stored")
        s_spill, s_back, s_clear = sem("x_spilled"), sem("x_back"), sem("block_diagonals_cleared")

        L = range(LAYERS)
        DI = [(d, i) for d in range(2) for i in range(2)]
        BATCH = 11

        def layer_keys(fn):
            return [(l,) + k for l in L for k in fn()]

        def k_rp():
            out = []
            for i in range(2):
                out += [("ksq", i), ("vt", i)]
            for d in range(2):
                out += [("sample", d, 0), ("lora", d, 0)]
                for i in range(2):
                    for s in range(BATCH):
                        for f in range(2):
                            out += [("b", d, i, s, f)]
                            if (i, s, f) == (0, 7, 1):
                                out += [("sample", d, 1), ("lora", d, 1)]
                out += [("chain", d, s) for s in range(2, 8)]
                out += [(n, d, i) for n in ("read", "mean", "var") for i in range(2)]
            return out + [("bonus", i) for i in range(2)]

        def k_ra():
            out = [("kroot", i) for i in range(2)] + [("tanh",)]
            exps = lambda d, i: [(n, d, i) for n in ("expE", "expL", "expN")]
            for d in range(2):
                out += [("sig", d, 0)] + exps(d, 0)
                for i in range(2):
                    out += [("bdf", d, i)]
                    for s in range(BATCH):
                        for f in range(2):
                            out += [("b", d, i, s, f)]
                            if (i, s, f) == (0, 8, 0):
                                out += [("sig", d, 1)]
                            if (i, s, f) == (0, 9, 1):
                                out += exps(d, 1)
                out += [(n, d, i) for n in ("osq", "oroot") for i in range(2)]
            return out

        def k_rv():
            out = []
            for i in range(2):
                out += [("ksq", i), ("kmax", i), ("vt", i), ("kk", i)]
            for d in range(2):
                out += [("cum", d, 0), ("keys", d, 0)]
                for i in range(2):
                    out += [("alpha", d, i), ("beta", d, i), ("feat", d, i)]
                    for s in range(BATCH):
                        for f in range(2):
                            if s in (5, 9):
                                out += [("first", d, i, s, f)]
                            out += [("b", d, i, s, f)]
                            if (i, s, f) == (0, 8, 1):
                                out += [("cum", d, 1)]
                            if (i, s, f) == (0, 9, 1):
                                out += [("keys", d, 1)]
                out += [("state", d, s) for s in range(1, 8)]
                out += [(n, d, i) for n in ("oread", "ocen", "onorm") for i in range(2)]
            for i in range(2):
                out += [("rk", i), ("done", i)]
            return out

        def k_hp():
            out = [("f1",), ("f2",)]
            out += [("f3", 0)]
            for p in range(6):
                out += ([("f3", p + 1)] if p < 5 else []) + [("fabs", p)]
            out += [("kern", f) for f in range(6)] + [("tr", g) for g in range(6)]
            for o in range(2):
                out += [("dft", o, f) for f in range(6)]
                out += [("inv", o, t) for t in range(6 if o == 0 else 2)]
            return out

        def k_ha():
            return [("skip",), ("s1",), ("s2",)] + [("abs", p) for p in range(6)]

        def k_hv():
            out = [("a1",), ("a2",)]
            for p in range(6):
                out += [("win", p), ("eo", p)]
            out += [("norm",)] + [("kern", f) for f in range(6)] + [("tr", g) for g in range(6)]
            for o in range(2):
                out += [("dft", o, f) for f in range(6)]
                out += [("inv", o, t) for t in range(6 if o == 0 else 2)]
            return out

        rp, ra_, rv = (Events(sem(n), layer_keys(k)) for n, k in
                       (("rwkv_products", k_rp), ("rwkv_activated", k_ra), ("rwkv_vector", k_rv)))
        hp, ha, hv = (Events(sem(n), layer_keys(k)) for n, k in
                      (("hyena_products", k_hp), ("hyena_activated", k_ha), ("hyena_vector", k_hv)))

        def prm(name, i=0, rows=P):
            c = POFF[name] + i
            return par[0:rows, c:c + 1]

        def cs(name, p0=0, p1=P):
            return cst[p0:p1, COFF[name]:COFF[name] + dict(CCOLS)[name]]

        def mask(m):
            o = COFF["masks"] + CH * m
            return cst[:, o:o + CH].unsqueeze(1).broadcast_to([P, HB, CH])

        def eye_b(n=HB):
            return cs("eye").unsqueeze(1).broadcast_to([P, n, CH])

        def bank(b, n=512):
            return ps[:, b, 0:n]

        def units(b):
            return ps[:, b, 0:HALF].rearrange("p (c t) -> p c t", t=CH)

        def wide_units(b):
            return ps[:, b:b + 2, 0:HALF].rearrange("p b (c a t) -> p b c a t", a=2, t=CH)

        def mask3(m):
            o = COFF["masks"] + CH * m
            return cst[:, o:o + CH].unsqueeze(1).unsqueeze(1).broadcast_to([P, 2, HB // 2, CH])

        def half_cols(t, i, f):
            return t[:, i, f * HB:(f + 1) * HB, :]

        BLOCKS = [(slice(0, CH), 0), (slice(CH, P), 1)]

        def table(tab, kt, ft):
            if ft < 4:
                return tab[:, kt, P * ft:P * ft + P]
            return tab[:, kt, 256 * (ft - 4):256 * (ft - 4) + 256:2]

        def chain(d, s):
            out = [(s if d == 0 else 7 - s, 0)]
            if s < 4:
                out.append((8 + s if d == 0 else 11 - s, 1))
            return out

        def x_count(l, part):
            return 112 * l + {0: 0, 2: 48, 1: 64}[part]

        def use_base(l, part):
            return USES * l + [0, FF_USES, FF_USES + PROJ_TILES, FF_USES + PROJ_TILES + OUT_TILES][part]

        def ffn_tile(u):
            for b, (j0, nj) in enumerate(FF_BLOCKS):
                if u < 2 * nj:
                    return b, "in", j0 + u // 2, u % 2
                u -= 2 * nj
                if u < OUT_TILES:
                    return b, "out", u
                u -= OUT_TILES

        def tile_k(n):
            l, u = n // USES, n % USES
            u = u if u < FF_USES else u - (USES - FF_USES)
            if u < 0 or (FF_USES <= n % USES < USES - FF_USES):
                return KT
            t = ffn_tile(u)
            return FF_BLOCKS[t[0]][1] if t[1] == "out" else KT

        def tile_used(n):
            l, u = n // USES, n % USES
            f = 0 if u < FF_USES else 1
            if f == 0 or u >= USES - FF_USES:
                t = ffn_tile(u if f == 0 else u - (USES - FF_USES))
                if t[1] == "in":
                    return s_gu, (2 * l + f) * 2 * FT + 2 * t[2] + 2
                return s_fo, x_count(l, f) + 16 * t[0] + 2 * t[2] + 2
            u -= FF_USES
            if u < A_TILES + C_TILES:
                return s_pj, 2 * (14 * l + u) + 2
            if u < A_TILES + C_TILES + QK_TILES:
                return s_qk, 14 * l + u - 14 + 1
            if u < PROJ_TILES:
                return s_qk, 14 * (l + 1)
            u -= PROJ_TILES
            return s_fo, x_count(l, 2) + 2 * u + 2

        block = ctx.enter_context(nc.Block())

        @block.sync
        def _(sp):
            sp.dma_start(x[:, :, :], xT).then_inc(s_x, 16)
            sp.dma_start(cst[:, :], const_d).then_inc(s_const, 16)

            def load_tile(n):
                if n >= RAWS:
                    sp.wait_ge(s_w, n - RAWS + 1)
                k = tile_k(n) * P
                sp.dma_start(wring[:, n % RAWS, :, :].rearrange("p k m -> p (k m)")[:, 0:k],
                             wa[n // USES, n % USES][:, 0:k]).then_inc(s_wa[n % RAWS], 16)

            for l in L:
                if l:
                    sp.wait_ge(s_h, 8 * 4 * l)
                sp.dma_start(par[:, :], par_d[l]).then_inc(s_par, 16)
                sp.dma_start(small[:, :], small_d[l]).then_inc(s_par, 16)
                for u in range(FF_USES + 3):
                    load_tile(USES * l + u)
                sp.wait_ge(s_xup, x_count(l, 0) + 48)
                sp.dma_start(outT, x[:, :, :]).then_inc(s_spill, 16)
                for u in range(FF_USES + 3, FF_USES + A_TILES + RAWS):
                    load_tile(USES * l + u)
                sp.wait_ge(s_spill, 16 * (l + 1))
                sp.wait_ge(*rv.at(l, "b", 1, 1, BATCH - 1, 1))
                sp.dma_start(x[:, :, :], outT).then_inc(s_back, 16)
                for u in range(FF_USES + A_TILES + RAWS, FF_USES + PROJ_TILES + RAWS):
                    load_tile(USES * l + u)
                sp.wait_ge(s_g4, 6 * l + 4)
                sp.dma_start(hwt[:, :], hw_d[l]).then_inc(s_hz, 16)
                for t, n, loaded in ((hz, "z", s_hz), (hdecay, "decay", s_hz), (hcos, "cos", s_hy), (hsin, "sin", s_hy)):
                    flat = t[:, :, :].rearrange("p a b -> p (a b)") if len(t.shape) == 3 else t[:, :]
                    sp.dma_start(flat, hy_d[:, HOFF[n]:HOFF[n] + dict(HCOLS)[n]]).then_inc(loaded, 16)
                sp.dma_start(altrow[:, :], hy_d[0:1, HOFF["altrow"]:HOFF["altrow"] + 512]).then_inc(s_hy, 16)
                for u in range(FF_USES + PROJ_TILES + RAWS, USES):
                    load_tile(USES * l + u)
            sp.wait_ge(s_fin, 1)
            sp.dma_start(outT, hout[:, :, :]).then_inc(s_out, 16)
            sp.wait_ge(s_out, 16)

        @block.gpsimd
        def _(pool):
            for l in L:
                def clear(t):
                    return pool.memset(t[:, :, :, :].rearrange("p c a t -> p (c a t)"), 0.0)

                pool.wait_ge(s_spill, 16 * (l + 1))
                pool.wait_ge(s_h, 8 * (4 * l + 2))
                for t in (Na_bd, Ma_bd, No_bd, G_bd, vbd, btok_bd):
                    clear(t)
                pool.wait_ge(s_pj, 28 * l + 2 * A_TILES)
                clear(ktok_bd)
                clear(Mb_bd).then_inc(s_clear, 1)

        @block.tensor
        def _(pe):
            norms = [0]
            gns = [0]

            def mm(out, lhsT, rhs, start=True, stop=True):
                return pe.matmul(out, lhsT, rhs, start=start, stop=stop)

            def mm3(out, lhs, rhs, start, stop):
                mm(out, lhs[0], rhs[0], start, False)
                mm(out, lhs[0], rhs[1], False, False)
                return mm(out, lhs[1], rhs[0], False, stop)

            def norm():
                pe.wait_ge(s_acc, 7 * (norms[0] + 1))
                for f in range(2):
                    mm(bank(6 + f, HALF), cs("ones"), rstd[:, f * HALF:(f + 1) * HALF]).then_inc(s_sum, 1)
                norms[0] += 1

            def tile_in(n):
                pe.wait_ge(s_w, n + 1)
                return wh[:, n % SPLITS, :, :], wl[:, n % SPLITS, :, :]

            def w_k(w, c):
                return w[0][:, c, :], w[1][:, c, :]

            def h_k(c, cols):
                return hh[:, c, cols], hl[:, c, cols]

            hmade = [0]

            def ffn(l, f):
                n = use_base(l, 3 if f else 0)
                u0 = (2 * l + f) * 2 * FT
                hbase = KT * hmade[0]
                hmade[0] += 1
                for b, (j0, nj) in enumerate(FF_BLOCKS):
                    for j in range(j0, j0 + nj):
                        w = tile_in(n), tile_in(n + 1)
                        n += 2
                        for hf_ in range(2):
                            unit = u0 + 2 * j + hf_
                            if unit >= 2:
                                pe.wait_ge(s_mul, unit - 1)
                            cols = slice(hf_ * HALF, (hf_ + 1) * HALF)
                            for side in range(2):
                                for c in range(KT):
                                    if j == 0 and hf_ == 0 and side == 0:
                                        pe.wait_ge(s_h, hbase + c + 1)
                                    m = mm3(bank(2 * (unit % 2) + side, HALF), w_k(w[side], c), h_k(c, cols),
                                            c == 0, c == KT - 1)
                            m.then_inc(s_gu, 1)
                    for m_ in range(OUT_TILES):
                        w = tile_in(n)
                        n += 1
                        for hf_ in range(2):
                            v = 16 * b + 2 * m_ + hf_
                            if v >= 4:
                                pe.wait_ge(s_xup, x_count(l, f) + v - 3)
                            cols = slice(hf_ * HALF, (hf_ + 1) * HALF)
                            for k in range(nj):
                                if m_ == 0:
                                    pe.wait_ge(s_act, u0 + 2 * (j0 + k) + hf_ + 1)
                                m = mm3(bank(4 + v % 4, HALF), w_k(w, k), (ah[:, k, cols], al_[:, k, cols]),
                                        k == 0, k == nj - 1)
                            m.then_inc(s_fo, 1)

            def proj(l, i):
                w = tile_in(use_base(l, 1) + i)
                pi = 14 * l + i
                if pi >= 2:
                    pe.wait_ge(s_raw, 2 * (pi - 1))
                if i in (0, A_TILES):
                    hbase = KT * hmade[0]
                    hmade[0] += 1
                for s, (t0, tn) in enumerate(SEGS):
                    for c in range(KT):
                        if i in (0, A_TILES) and s == 0:
                            pe.wait_ge(s_h, hbase + c + 1)
                        m = mm3(bank(2 * (pi % 2) + s, tn), w_k(w, c), h_k(c, slice(t0, t0 + tn)), c == 0, c == KT - 1)
                    m.then_inc(s_pj, 1)

            def both(b, lhs, rhs, lhs2=None, rhs2=None):
                for c in range(HB):
                    o = ps[:, b, CH * c:CH * c + CH]
                    m = mm(o, lhs(c), rhs(c), True, lhs2 is None)
                    if lhs2:
                        m = mm(o, lhs2(c), rhs2(c), False, True)
                return m

            def wide(b, lhs, rhs):
                for c in range(HB):
                    m = mm(ps[:, b + c // 3, P * (c % 3):P * (c % 3) + P], lhs(c), rhs(c).rearrange("p a t -> p (a t)"))
                return m

            def batch(l, d, i, s, f):
                c0, o = f * HB, 4 * f
                D = lambda t: (lambda c: t[:, c0 + c, :, :].rearrange("p a t -> p (a t)"))
                B = lambda t: (lambda c: t[:, c0 + c, :])
                arr = lambda c: ar[:, c0 + c, :, :]
                vv = lambda c: vtok[:, i, c0 + c, :]
                RR = lambda c: R[:, c0 + c, :, :]
                QQ = lambda c: Q[f][:, c, :, :]
                Q1 = lambda c: Q[f][:, c, 1, :]
                ey = lambda c: cs("eye")
                if s:
                    pe.wait_ge(*rv.at(l, "b", d, i, s - 1, f))
                    pe.wait_ge(*ra_.at(l, "b", d, i, s - 1, f))
                if s == 0:
                    both(o, D(alpha_bd), B(beta))
                    wide(o + 1, D(beta_bd), arr)
                    m = both(o + 3, D(beta_bd), ey)
                elif s == 1:
                    wide(o, D(kap_bd), arr)
                    both(o + 2, D(kap_bd), ey)
                    m = both(o + 3, D(alpha_bd), ey)
                elif s == 2:
                    both(o + 1, D(Ma_bd), B(Na))
                    both(o + 2, D(Na_bd), B(Ma))
                    m = both(o, D(Lak_bd), vv)
                elif s == 3:
                    both(o + 1, D(Mb_bd), B(Nb))
                    m = wide(o + 2, D(Nb_bd), lambda c: Mb_X[:, c0 + c, :, :])
                elif s == 4:
                    both(o + 1, D(Ma_bd), B(Na))
                    m = both(o, D(Na_bd), B(X))
                elif s == 5:
                    m = both(o, D(Nb_bd), B(X))
                elif s == 6:
                    both(o, D(No_bd), B(X))
                    both(o + 1, D(X_bd), B(No))
                    m = wide(o + 2, D(X_bd), RR)
                elif s == 7:
                    m = both(o, D(Na_bd), B(Ma))
                elif s == 8:
                    if (i, f) == (0, 1):
                        pe.wait_ge(*ra_.at(l, "sig", d, 1))
                    m = wide(o, D(Mb_bd), QQ)
                elif s == 9:
                    m = wide(o + 2, D(Ma_bd), RR)
                else:
                    wide(o, D(Q0_bd), lambda c: btok_Mrb[:, c0 + c, :, :])
                    both(o + 2, D(btok_bd), Q1, D(ktok_bd), vv)
                    m = both(o + 3, D(Q1_bd), B(Mrb), D(vbd), B(Mrk))
                m.then_inc(*rp.inc(l, "b", d, i, s, f))

            def lora(l, d, i):
                wr, arow = slice(32 * d, 32 * d + 32), slice(64 + 32 * d, 96 + 32 * d)
                lo = SOFF["lora"] + P * i
                mm(ps[:, 7, 0:DEC], small[wr, lo:lo + P], pa[wr, 6, SEQ:T]).then_inc(*rp.inc(l, "sample", d, i))
                mm(bank(5), small[wr, lo:lo + P], pa[wr, 6, 0:SEQ])
                mm(bank(6), small[arow, lo:lo + P], pa[arow, 6, 0:SEQ])
                pe.wait_ge(*rp.at(l, "sample", d, i))
                mm(ps[:, 7, DEC:2 * DEC], small[arow, lo:lo + P], pa[arow, 6, SEQ:T]).then_inc(*rp.inc(l, "lora", d, i))

            def rwkv(l):
                blk = cs("blk")
                for i in range(2):
                    pe.wait_ge(*rv.at(l, "ksq", i))
                    for s, (t0, tn) in enumerate(SEGS):
                        m = mm(bank(s, tn), blk, tmp[:, 1, t0:t0 + tn])
                    m.then_inc(*rp.inc(l, "ksq", i))
                    for f in range(2):
                        for c in range(HB):
                            for hd in range(2):
                                r = slice(64 * hd, 64 * hd + 64)
                                t0 = (f * HB + c) * CH
                                m = mm(ps[r, 2 + f, CH * c:CH * c + CH], pa[r, 4 + i, t0:t0 + CH], cs("eye")[r, :])
                    m.then_inc(*rp.inc(l, "vt", i))
                    pe.wait_ge(*rv.at(l, "kk", i))
                pe.wait_ge(*ra_.at(l, "tanh"))
                for d in range(2):
                    if d:
                        pe.wait_ge(*ra_.at(l, "oroot", 0, 1))
                    lora(l, d, 0)
                    for i in range(2):
                        pe.wait_ge(*rv.at(l, "feat", d, i))
                        pe.wait_ge(*ra_.at(l, "bdf", d, i))
                        for s in range(BATCH):
                            for f in range(2):
                                batch(l, d, i, s, f)
                                if (i, s, f) == (0, 7, 1):
                                    lora(l, d, 1)
                        for f in range(2):
                            pe.wait_ge(*rv.at(l, "b", d, i, BATCH - 1, f))
                            pe.wait_ge(*ra_.at(l, "b", d, i, BATCH - 1, f))
                    for s in range(2, 8):
                        pe.wait_ge(*rv.at(l, "state", d, s - 1))
                        for i in range(2):
                            for c, col in chain(d, s - 1):
                                for hd in range(2):
                                    r = slice(64 * hd, 64 * hd + 64)
                                    m = mm(ps[r, 0, (2 * i + col) * CH:(2 * i + col + 1) * CH], trans[r, i, c, :],
                                           state[r, i, c, :])
                        m.then_inc(*rp.inc(l, "chain", d, s))
                    pe.wait_ge(*rv.at(l, "state", d, 7))
                    for i in range(2):
                        for f in range(2):
                            c0 = f * HB
                            for c in range(HB):
                                for hd in range(2):
                                    r = slice(64 * hd, 64 * hd + 64)
                                    m = mm(ps[r, 2 * i + f, CH * c:CH * c + CH], state[r, i, c0 + c, :],
                                           query[r, i, c0 + c, :])
                        m.then_inc(*rp.inc(l, "read", d, i))
                    for i in range(2):
                        pe.wait_ge(*rv.at(l, "oread", d, i))
                        for f in range(2):
                            m = mm(units(4 + 2 * i + f), blk, half_cols(olocal, i, f))
                        m.then_inc(*rp.inc(l, "mean", d, i))
                    for i in range(2):
                        pe.wait_ge(*ra_.at(l, "osq", d, i))
                        for f in range(2):
                            m = mm(bank(2 * i + f, HALF), blk, tmp[:, 2 * i, f * HALF:(f + 1) * HALF])
                        m.then_inc(*rp.inc(l, "var", d, i))
                for i in range(2):
                    pe.wait_ge(*rv.at(l, "rk", i))
                    for s, (t0, tn) in enumerate(SEGS):
                        mm(bank(s, tn), blk, tmp[:, 0, t0:t0 + tn])
                        lo = SOFF["g_up"] + P * i
                        m = mm(bank(2 + s, tn), small[0:64, lo:lo + P], pa[0:64, 7, t0:t0 + tn])
                    m.then_inc(*rp.inc(l, "bonus", i))

            def gnorm():
                pe.wait_ge(s_g1, gns[0] + 1)
                if gns[0] > 1:
                    pe.wait_ge(s_g3, gns[0] - 1)
                for f in range(2):
                    m = mm(bank(2 * (gns[0] % 2) + f, HALF), cs("blk"), sqb[:, gns[0] % 2, f * HALF:(f + 1) * HALF])
                m.then_inc(s_g2, 1)
                gns[0] += 1

            def filters(l):
                pe.wait_ge(s_hz, 48 * (l + 1))
                for s, (t0, tn) in enumerate(SEGS):
                    mm(ps[0:64, s, 0:tn], hwt[0:33, 0:64], hz[0:33, t0:t0 + tn])
                mm(bank(2), cs("ones", 0, 1), hwt[0:1, HWOFF["skip"]:HWOFF["skip"] + 512]).then_inc(*hp.inc(l, "f1"))
                pe.wait_ge(*ha.at(l, "s1"))
                for s, (t0, tn) in enumerate(SEGS):
                    m = mm(ps[0:64, s, 0:tn], hwt[0:64, 64:128], h1[0:64, t0:t0 + tn])
                m.then_inc(*hp.inc(l, "f2"))
                pe.wait_ge(*ha.at(l, "s2"))
                def taps(p):
                    if p > 1:
                        pe.wait_ge(*hv.at(l, "win", p - 2))
                    for dr in range(2):
                        lo = HWOFF["w3"] + 512 * dr
                        m = mm(bank(4 * (p % 2) + dr), h1[0:64, P * p:P * p + P], hwt[0:64, lo:lo + 512])
                    m.then_inc(*hp.inc(l, "f3", p))

                taps(0)
                for p in range(6):
                    if p < 5:
                        taps(p + 1)
                    pe.wait_ge(*ha.at(l, "abs", p))
                    s, k = (0, p) if p < 4 else (1, p - 4)
                    mm(bank(6 + s), cs("ones"), af[:, :], k == 0, False)
                    mm(bank(6 + s), cs("ones"), ab[:, :], False, k == (3 if s == 0 else 1)).then_inc(*hp.inc(l, "fabs", p))
                pe.wait_ge(*hv.at(l, "eo", 5))
                pe.wait_ge(s_hy, 48 * (l + 1))
                for ft in range(6):
                    if ft > 1:
                        pe.wait_ge(*hv.at(l, "kern", ft - 2))
                    b = 4 * (ft % 2)
                    s, kts = (0, 4) if ft < 4 else (1, 2)
                    for kt in range(kts):
                        mm(bank(b), table(hcos, kt, ft), se[:, 4 * s + kt, :], kt == 0, kt == kts - 1)
                    for kt in range(kts):
                        m = mm(bank(b + 1), table(hsin, kt, ft), so[:, 4 * s + kt, :], kt == 0, kt == kts - 1)
                    if ft in (0, 4):
                        for kt in range(kts):
                            m = mm(ps[0:1, 2, :], cs("alt"), se[:, 4 * s + kt, :], kt == 0, kt == kts - 1)
                    m.then_inc(*hp.inc(l, "kern", ft))

            def hyena(l):
                for g in range(6):
                    if g >= 2:
                        pe.wait_ge(*hv.at(l, "tr", g - 2))
                    for j in range(4):
                        m = pe.transpose(ps[:, 4 + g % 2, P * j:P * j + P], conv[:, j, P * g:P * g + P], cs("ident"))
                    m.then_inc(*hp.inc(l, "tr", g))
                for o in range(2):
                    if o == 0:
                        pe.wait_ge(*hv.at(l, "tr", 5))
                    src = vt if o == 0 else zt
                    for ft in range(6):
                        if ft >= 2:
                            pe.wait_ge(*hv.at(l, "dft", o, ft - 2))
                        s, kts = (0, 4) if ft < 4 else (1, 2)
                        for half, tab in ((0, hcos), (1, hsin)):
                            for kt in range(kts):
                                m = mm(ps[:, ft % 2, 256 * half:256 * half + 256], table(tab, kt, ft), src[:, 4 * s + kt, :],
                                       kt == 0, kt == kts - 1)
                        if ft in (0, 4):
                            for kt in range(kts):
                                m = mm(ps[0:1, 2, 0:256], cs("alt"), src[:, 4 * s + kt, :], kt == 0, kt == kts - 1)
                        m.then_inc(*hp.inc(l, "dft", o, ft))
                    pe.wait_ge(*hv.at(l, "dft", o, 5))
                    if o == 0:
                        for tt in range(6):
                            if tt >= 2:
                                pe.wait_ge(*hv.at(l, "inv", 0, tt - 2))
                            s, kts = (0, 4) if tt < 4 else (1, 2)
                            out = ps[:, 4 + tt % 2, 0:256]
                            for kt in range(kts):
                                mm(out, table(hcos, kt, tt), yc[:, 4 * s + kt, :], kt == 0, False)
                                mm(out, table(hsin, kt, tt), ys[:, 4 * s + kt, :], False, False)
                            mm(out, altrow[0:1, 0:P], xnyq[0:1, s, :], False, True).then_inc(*hp.inc(l, "inv", 0, tt))
                        pe.wait_ge(*hv.at(l, "inv", 0, 5))
                    else:
                        for i in range(2):
                            if i:
                                pe.wait_ge(*hv.at(l, "inv", 1, 0))
                            for s, (t0, tn) in enumerate(SEGS):
                                kts = 4 if s == 0 else 2
                                out = bank(4 + s, tn)
                                for kt in range(kts):
                                    for tab, y in ((hcos, yc), (hsin, ys)):
                                        rhs = tab[:, kt, :] if s == 0 else tab[:, kt, 0:512:2]
                                        mm(out, y[:, 4 * s + kt, P * i:P * i + P], rhs, kt == 0 and tab is hcos, False)
                                m = mm(out, xnyq[0:1, s, P * i:P * i + P], altrow[0:1, 0:tn], False, True)
                            m.then_inc(*hp.inc(l, "inv", 1, i))
                for i in range(2):
                    gnorm()

            def attention(l):
                for g in range(16):
                    if 16 * l + g >= 2:
                        pe.wait_ge(s_bv, 16 * l + g - 1)
                    for k in range(4):
                        lo = COFF["shift"] + 63 - (4 * g + k)
                        for half in range(2):
                            m = mm(ps[64 * half:64 * half + 64, 4 + g % 2, 120 * k:120 * k + 120], cst[0:31, lo:lo + 64],
                                   small[0:31, SOFF["rpb"]:SOFF["rpb"] + 120])
                    m.then_inc(s_bp, 1)
                pe.wait_ge(s_bv, 16 * (l + 1))

                def scores(u):
                    hd, i = u // 6, u % 6
                    r = slice(64 * (hd % 2), 64 * (hd % 2) + 64)
                    k0, kn = (0, 512) if i < 4 else (512, 256)
                    n = 48 * l + u
                    if n >= 2:
                        pe.wait_ge(s_sm, n - 1)
                    mm(bank(u % 2, kn), qT[r, hd // 2, P * i:P * i + P], kT[r, hd // 2, k0:k0 + kn]).then_inc(s_sc, 1)

                def turn(u):
                    n = 48 * l + u
                    pe.wait_ge(s_pn, n + 1)
                    if n >= 2:
                        pe.wait_ge(s_tc, n - 1)
                    for k in range(4 if u % 6 < 4 else 2):
                        m = pe.transpose(ps[:, 2 + u % 2, P * k:P * k + P], sc[:, u % SCB, P * k:P * k + P], cs("ident"))
                    m.then_inc(s_tr, 1)

                def weigh(hd):
                    r = slice(64 * (hd % 2), 64 * (hd % 2) + 64)
                    pe.wait_ge(s_tc, 48 * l + 6 * hd + 6)
                    if hd >= 1:
                        pe.wait_ge(s_pvc, 8 * l + hd)
                    slot = (use_base(l, 1) + A_TILES + C_TILES + QK_TILES + hd // 2) % SPLITS
                    v0 = P * slot + HD * (hd % 2)
                    for k in range(4):
                        mm(ps[r, 4, :], vta[:, k, v0:v0 + HD], pTp[hd % 2][:, k, :], k == 0, k == 3)
                    for k in range(2):
                        m = mm(ps[r, 5, 0:256], vta[:, 4 + k, v0:v0 + HD], pTs[hd % 2][:, k, :], k == 0, k == 1)
                    m.then_inc(s_pv, 1)

                for u in range(48 + LAG + 1):
                    if u < 48:
                        scores(u)
                    if LAG <= u < 48 + LAG:
                        turn(u - LAG)
                    if u > LAG and (u - LAG) % 6 == 0:
                        weigh((u - LAG) // 6 - 1)
                for i in range(4):
                    gnorm()

            def qkv(l):
                for i in range(QK_TILES):
                    w = tile_in(use_base(l, 1) + A_TILES + C_TILES + i)
                    if i >= 2:
                        pe.wait_ge(s_qkc, 14 * l + i - 1)
                    for s, (t0, tn) in enumerate(SEGS):
                        for c in range(KT):
                            m = mm3(bank(2 * (i % 2) + s, tn), w_k(w, c), h_k(c, slice(t0, t0 + tn)), c == 0, c == KT - 1)
                    m.then_inc(s_qk, 1)
                pe.wait_ge(s_qkc, 14 * l + 8)
                assert SPLITS == V_TILES
                for i in range(V_TILES):
                    tile_in(use_base(l, 1) + A_TILES + C_TILES + QK_TILES + i)
                for tt in range(6):
                    if tt >= 2:
                        pe.wait_ge(s_qkc, 14 * l + 8 + tt - 1)
                    for c in range(KT):
                        m = mm3(bank(tt % 2).rearrange("p (j m) -> p j m", m=P), h_k(c, slice(P * tt, P * tt + P)),
                                (wh[:, :, c, :], wl[:, :, c, :]), c == 0, c == KT - 1)
                    m.then_inc(s_qk, 1)
                pe.wait_ge(s_qkc, 14 * (l + 1))

            def mix_out(l):
                for m_ in range(OUT_TILES):
                    w = tile_in(use_base(l, 2) + m_)
                    for f in range(2):
                        v = 2 * m_ + f
                        if v >= 4:
                            pe.wait_ge(s_xup, x_count(l, 2) + v - 3)
                        cols = slice(f * HALF, (f + 1) * HALF)
                        for k in range(OUT_TILES):
                            if v == 0:
                                pe.wait_ge(s_m, 8 * l + k + 1)
                            m = mm3(bank(v % 4, HALF), w_k(w, k), (mh[:, k, cols], ml[:, k, cols]), k == 0, k == 7)
                        m.then_inc(s_fo, 1)

            pe.wait_ge(s_const, 16)
            for l in L:
                pe.wait_ge(s_par, 32 * (l + 1))
                norm()
                ffn(l, 0)
                norm()
                for i in range(A_TILES):
                    proj(l, i)
                rwkv(l)
                for i in range(C_TILES):
                    proj(l, A_TILES + i)
                pe.wait_ge(s_raw, 28 * (l + 1))
                qkv(l)
                attention(l)
                filters(l)
                pe.wait_ge(*hv.at(l, "kern", 5))
                hyena(l)
                mix_out(l)
                norm()
                ffn(l, 1)
            norm()

        @block.scalar
        def _(sa):
            A = sa.activation
            norms = [0]
            gns = [0]

            steps = [0]

            def inverse_root(dst, parts, bias, scale):
                for cols, src in parts:
                    m = A(dst[:, cols], src, ACT.Ln, bias=bias, scale=scale)
                m.then_inc(s_astep, 1)
                steps[0] += 1
                sa.wait_ge(s_astep, steps[0])
                return A(dst, dst, ACT.Exp, scale=-0.5)

            def use_log_exp():
                sa.preload_act_table_set("natural_log_exp_and_others")

            def halves(b):
                return [(slice(f * HALF, (f + 1) * HALF), bank(b + f, HALF)) for f in range(2)]

            split = [0]

            def split_to(n):
                while split[0] <= min(n, LAYERS * USES - 1):
                    t = split[0]
                    sa.wait_ge(s_wa[t % RAWS], 16 * (t // RAWS + 1))
                    if t >= SPLITS:
                        sa.wait_ge(*tile_used(t - SPLITS))
                    k = tile_k(t)
                    sa.copy(wh[:, t % SPLITS, 0:k, :], wring[:, t % RAWS, 0:k, :]).then_inc(s_whi, 1)
                    split[0] += 1

            def square(m, ready):
                if ready:
                    sa.wait_ge(s_xup, ready)
                if m >= 2:
                    sa.wait_ge(s_acc, 7 * norms[0] + max(m - 2, 1))
                A(sqb[:, m % 2, :], x[:, m, :], ACT.Square).then_inc(s_sq, 1)

            hmade = [0]

            def high_h():
                for c in range(KT):
                    n = KT * hmade[0] + c
                    sa.wait_ge(s_ht, n + 1)
                    sa.copy(hh[:, c, :], sqb[:, c % 2, :]).then_inc(s_hhi, 1)
                hmade[0] += 1

            def norm():
                use_log_exp()
                sa.wait_ge(s_sum, 2 * norms[0] + 2)
                inverse_root(rstd[:, :], halves(6), eps[:, 0:1], 1.0 / D).then_inc(s_root, 1)
                norms[0] += 1

            def ffn(l, f, cap):
                n = use_base(l, 3 if f else 0)
                for b, (j0, nj) in enumerate(FF_BLOCKS):
                    for j in range(j0, j0 + nj):
                        split_to(min(n + 3, cap))
                        n += 2
                        for hf_ in range(2):
                            u = (2 * l + f) * 2 * FT + 2 * j + hf_
                            sa.wait_ge(s_gu, u + 1)
                            if u >= 2:
                                sa.wait_ge(s_mul, u - 1)
                            A(silu[:, u % 2, :], bank(2 * (u % 2), HALF), ACT.Silu).then_inc(s_silu, 1)
                            if b and j == j0 and hf_ == 0:
                                sa.wait_ge(s_fo, x_count(l, f) + 16 * b)
                            sa.wait_ge(s_mul, u + 1)
                            sa.copy(ah[:, j - j0, hf_ * HALF:(hf_ + 1) * HALF], gated[:, u % 2, :]).then_inc(s_ahi, 1)
                    for m in range(OUT_TILES):
                        split_to(min(n + 2, cap))
                        n += 1
                        if b == 2 and m:
                            square(m - 1, x_count(l, f) + 32 + 2 * m)
                square(OUT_TILES - 1, x_count(l, f) + 48)

            def copy_raw(l, i, bufs, cap):
                pi = 14 * l + i
                split_to(min(use_base(l, 1) + i + 2, cap))
                for s, (t0, tn) in enumerate(SEGS):
                    sa.wait_ge(s_pj, 2 * pi + s + 1)
                    if pi >= 2 and s == 0:
                        sa.wait_ge(s_mixd, pi - 1)
                    sa.copy(bufs[pi % 2][:, 1 + t0 + s:1 + t0 + s + tn], bank(2 * (pi % 2) + s, tn)).then_inc(s_raw, 1)

            def sigmoids(l, d, i):
                sa.wait_ge(*rp.at(l, "lora", d, i))
                if i:
                    sa.wait_ge(*rv.at(l, "feat", d, 0))
                w0, a0 = prm("rwkv_w0", 2 * d + i), prm("rwkv_a0", 2 * d + i)
                A(tmp[:, 0, 0:SEQ], bank(5), ACT.Sigmoid, bias=w0)
                A(tmp[:, 1, 0:SEQ], bank(6), ACT.Sigmoid, bias=a0)
                A(tmp[:, 0, SEQ:T], ps[:, 7, 0:DEC], ACT.Sigmoid, bias=w0)
                A(tmp[:, 1, SEQ:T], ps[:, 7, DEC:2 * DEC], ACT.Sigmoid, bias=a0).then_inc(*ra_.inc(l, "sig", d, i))

            def exps(l, d, i):
                use_log_exp()
                sa.wait_ge(*rv.at(l, "cum", d, i))
                A(tmp[:, 0, :], tmp[:, 0, :], ACT.Exp).then_inc(*ra_.inc(l, "expE", d, i))
                A(tmp[:, 3, :], tmp[:, 2, :], ACT.Exp).then_inc(*ra_.inc(l, "expL", d, i))
                A(tmp[:, 2, :], tmp[:, 2, :], ACT.Exp, scale=-1.0).then_inc(*ra_.inc(l, "expN", d, i))

            def batch(l, d, i, s, f):
                k, o = (l, "b", d, i), 4 * f
                h = slice(f * HB, (f + 1) * HB)

                def diagonal(dst, src, blocks=BLOCKS):
                    for r, a in blocks:
                        m = sa.copy(dst[r, h, a, :], src[r, :, :])
                    return m

                def minus(dst, b):
                    return A(dst, units(b), ACT.Copy, scale=-1.0)

                if s == 1:
                    sa.wait_ge(*rv.at(*k, 0, f))
                    diagonal(Na_bd, Na[:, h, :])
                    diagonal(Ma_bd, Ma[:, h, :])
                elif s == 5:
                    diagonal(No_bd, No[:, h, :])
                sa.wait_ge(*rp.at(*k, s, f))
                if s == 0:
                    sa.copy(btok[:, h, :], units(o + 3))
                    m = diagonal(btok_bd, units(o + 3))
                elif s == 1:
                    diagonal(ktok_bd, units(o + 2))
                    m = minus(R[:, h, 0, :], o + 3)
                elif s == 2:
                    sa.copy(Nb[:, h, :], units(o + 1))
                    diagonal(Nb_bd, units(o + 1))
                    m = minus(R[:, h, 1, :], o)
                elif s == 3:
                    sa.copy(Na[:, h, :], units(o + 1))
                    m = diagonal(Na_bd, units(o + 1))
                elif s == 4:
                    m = diagonal(Nb_bd, units(o + 1))
                elif s == 5:
                    sa.wait_ge(*rv.at(l, "first", d, i, 5, f))
                    m = diagonal(X_bd, X[:, h, :], BLOCKS[1:])
                elif s == 6:
                    for b in range(2):
                        m = sa.copy(Q[f][:, 3 * b:3 * b + 3, :, :].rearrange("p c a t -> p (c a t)"), bank(o + 2 + b, HALF))
                elif s == 7:
                    m = diagonal(Mb_bd, units(o), BLOCKS[1:])
                elif s == 8:
                    m = diagonal(Ma_bd, Ma[:, h, :])
                elif s == 9:
                    sa.wait_ge(*rv.at(l, "first", d, i, 9, f))
                    m = diagonal(Q1_bd, Q[f][:, :, 1, :])
                else:
                    m = sa.copy(half_cols(olocal, i, f), units(o + 3))
                m.then_inc(*ra_.inc(*k, s, f))

            def rwkv(l):
                use_log_exp()
                for i in range(2):
                    sa.wait_ge(*rv.at(l, "kmax", i))
                    inverse_root(tmp[:, 2, :], [(slice(0, T), tmp[:, 2, :])], eps[:, 2:3], float(HD))\
                        .then_inc(*ra_.inc(l, "kroot", i))
                A(pa[0:64, 7, :], pa[0:64, 7, :], ACT.Sigmoid)
                A(pa[0:64, 6, :], pa[0:64, 6, :], ACT.Tanh).then_inc(*ra_.inc(l, "tanh"))
                for d in range(2):
                    if d:
                        sa.wait_ge(*rv.at(l, "onorm", 0, 1))
                    sigmoids(l, d, 0)
                    exps(l, d, 0)
                    for i in range(2):
                        if (d, i) == (0, 0):
                            sa.wait_ge(*rv.at(l, "kk", 1))
                            sa.wait_ge(s_clear, l + 1)
                        for r, a in BLOCKS:
                            sa.copy(vbd[r, :, a, :], vtok[r, i, :, :])
                        sa.wait_ge(*rv.at(l, "alpha", d, i))
                        for r, a in BLOCKS:
                            sa.copy(alpha_bd[r, :, a, :], ar[r, :, 0, :])
                        sa.wait_ge(*rv.at(l, "beta", d, i))
                        for r, a in BLOCKS:
                            m = sa.copy(beta_bd[r, :, a, :], beta[r, :, :])
                        m.then_inc(*ra_.inc(l, "bdf", d, i))
                        for s in range(BATCH):
                            for f in range(2):
                                batch(l, d, i, s, f)
                                if (i, s, f) == (0, 8, 0):
                                    sigmoids(l, d, 1)
                                if (i, s, f) == (0, 9, 1):
                                    exps(l, d, 1)
                    for i in range(2):
                        sa.wait_ge(*rv.at(l, "ocen", d, i))
                        A(tmp[:, 2 * i, :], olocal[:, i, :, :].rearrange("p c t -> p (c t)"), ACT.Square)\
                            .then_inc(*ra_.inc(l, "osq", d, i))
                    for i in range(2):
                        sa.wait_ge(*rp.at(l, "var", d, i))
                        inverse_root(tmp[:, 2 * i + 1, :], halves(2 * i), eps[:, 1:2], 1.0).then_inc(*ra_.inc(l, "oroot", d, i))

            def gn(tile):
                n = gns[0]
                if n > 1:
                    sa.wait_ge(s_g4, n - 1)
                A(sqb[:, n % 2, :], mixed[:, tile, :], ACT.Square).then_inc(s_g1, 1)
                gns[0] += 1

            def gn_root(n):
                sa.wait_ge(s_g2, n + 1)
                inverse_root(sqb[:, n % 2, :], halves(2 * (n % 2)), eps[:, 0:1], 1.0).then_inc(s_g3, 1)

            def filters(l):
                sa.wait_ge(*hp.at(l, "f1"))
                sa.copy(skipb[:, :], bank(2)).then_inc(*ha.inc(l, "skip"))
                for n in (1, 2):
                    sa.wait_ge(*hv.at(l, f"a{n}"))
                    A(h1[0:64, :], arg[0:64, :], ACT.Sin).then_inc(*ha.inc(l, f"s{n}"))
                for p in range(6):
                    sa.wait_ge(*hv.at(l, "win", p))
                    if p:
                        sa.wait_ge(*hp.at(l, "fabs", p - 1))
                    A(af[:, :], hf[:, :], ACT.Abs)
                    A(ab[:, :], hb[:, :], ACT.Abs).then_inc(*ha.inc(l, "abs", p))

            def qkv(l, cap):
                for i in range(QK_TILES):
                    split_to(min(use_base(l, 1) + A_TILES + C_TILES + i + 2, cap))
                    sa.wait_ge(s_qk, 14 * l + i + 1)
                    dst = qT if i < 4 else kT
                    for s, (t0, tn) in enumerate(SEGS):
                        m = sa.copy(dst[:, i % 4, t0:t0 + tn], bank(2 * (i % 2) + s, tn))
                    m.then_inc(s_qkc, 1)
                split_to(cap)
                for tt in range(6):
                    sa.wait_ge(s_qk, 14 * l + 8 + tt + 1)
                    sa.copy(vta[:, tt, :], bank(tt % 2)).then_inc(s_qkc, 1)

            def attention(l):
                def exps(u):
                    kn = 512 if u % 6 < 4 else 256
                    sa.wait_ge(s_sm, 48 * l + u + 1)
                    b = u % SCB
                    A(sc[:, b, 0:kn], sc[:, b, 0:kn], ACT.Exp, bias=nmax[:, b:b + 1],
                      accum_out=ssum[:, b:b + 1]).then_inc(s_pr, 1)

                def turned(u):
                    hd, i = u // 6, u % 6
                    sa.wait_ge(s_tr, 48 * l + u + 1)
                    if i == 0 and 8 * l + hd >= 2:
                        sa.wait_ge(s_pv, 8 * l + hd - 1)
                    if i < 4:
                        dst, kn = pTp[hd % 2][:, :, P * i:P * i + P], 4
                    else:
                        dst, kn = pTs[hd % 2][:, :, P * (i - 4):P * (i - 3)], 2
                    sa.copy(dst, ps[:, 2 + u % 2, 0:P * kn].rearrange("p (k q) -> p k q", q=P)).then_inc(s_tc, 1)

                def weighed(hd):
                    r = slice(64 * (hd % 2), 64 * (hd % 2) + 64)
                    sa.wait_ge(s_pv, 8 * l + hd + 1)
                    sa.copy(mixed[r, 2 + hd // 2, 0:512], ps[r, 4, :])
                    sa.copy(mixed[r, 2 + hd // 2, 512:768], ps[r, 5, 0:256]).then_inc(s_pvc, 1)

                for u in range(48 + LAG + 2):
                    if u < 48:
                        exps(u)
                    if LAG <= u < 48 + LAG:
                        turned(u - LAG)
                    if u > LAG + 1 and (u - LAG - 1) % 6 == 0:
                        weighed((u - LAG - 1) // 6 - 1)

            def high_mixed(l, tiles):
                for k in tiles:
                    sa.copy(mh[:, k, :], mixed[:, k, :]).then_inc(s_mhi, 1)

            def mix_out(l):
                sa.wait_ge(s_g4, 6 * (l + 1))
                last = use_base(l, 2)
                for k in range(OUT_TILES):
                    if k == 1:
                        split_to(last)
                    high_mixed(l, [k])
                for m in range(OUT_TILES):
                    split_to(last + m + 2)
                    if m:
                        square(m - 1, x_count(l, 2) + 2 * m)
                square(OUT_TILES - 1, x_count(l, 2) + 16)

            sa.wait_ge(s_eps, 1)
            sa.wait_ge(s_x, 16)
            for m in range(OUT_TILES):
                square(m, 0)
            for l in L:
                sa.wait_ge(s_par, 32 * (l + 1))
                cap_a = use_base(l, 1) + A_TILES - 1
                cap_b = use_base(l, 2) - 1
                norm()
                split_to(use_base(l, 0) + 1)
                high_h()
                ffn(l, 0, cap_a)
                norm()
                high_h()
                sa.wait_ge(s_zero, 2 * l + 1)
                for i in range(A_TILES):
                    copy_raw(l, i, raw, cap_a)
                sa.wait_ge(s_mixd, 14 * l + A_TILES)
                rwkv(l)
                sa.wait_ge(*rv.at(l, "done", 1))
                split_to(use_base(l, 1) + A_TILES)
                high_h()
                sa.wait_ge(s_zero, 2 * l + 2)
                for i in range(A_TILES, A_TILES + C_TILES):
                    copy_raw(l, i, hraw, cap_b)
                sa.wait_ge(s_mixd, 14 * (l + 1))
                qkv(l, cap_b)
                use_log_exp()
                attention(l)
                sa.wait_ge(s_pvc, 8 * (l + 1))
                for i in range(4):
                    gn(2 + i)
                    if i:
                        gn_root(6 * l + i - 1)
                gn_root(6 * l + 3)
                sa.wait_ge(s_g4, 6 * l + 4)
                filters(l)
                use_log_exp()
                for i in range(2):
                    sa.wait_ge(*hv.at(l, "inv", 1, i))
                    gn(6 + i)
                    gn_root(6 * l + 4 + i)
                mix_out(l)
                norm()
                high_h()
                ffn(l, 1, LAYERS * USES)
            norm()

        @block.vector
        def _(ve):
            norms = [0]
            gns = [0]
            steps = [0]
            TT, TS, STT = ve.tensor_tensor, ve.tensor_scalar, ve.scalar_tensor_tensor
            M, AD, SU = ALU.mult, ALU.add, ALU.subtract

            def step(ins):
                steps[0] += 1
                ins.then_inc(s_vstep, 1)
                ve.wait_ge(s_vstep, steps[0])

            split = [0]

            def split_to(n):
                while split[0] <= min(n, LAYERS * USES - 1):
                    t = split[0]
                    ve.wait_ge(s_whi, t + 1)
                    k = tile_k(t)
                    TT(wl[:, t % SPLITS, 0:k, :], wring[:, t % RAWS, 0:k, :], wh[:, t % SPLITS, 0:k, :].bitcast(F32), SU)\
                        .then_inc(s_w, 1)
                    split[0] += 1

            def add_squares(m):
                ve.wait_ge(s_sq, KT * norms[0] + m + 1)
                if m > 1:
                    ve.wait_ge(s_acc, 7 * norms[0] + m - 1)
                if m:
                    TT(rstd[:, :], sqb[:, 0, :] if m == 1 else rstd[:, :], sqb[:, m % 2, :], AD).then_inc(s_acc, 1)

            hmade = [0]

            def split_h(gain):
                base = KT * hmade[0]
                for c in range(KT + 1):
                    if c < KT:
                        if c >= 2:
                            ve.wait_ge(s_h, base + c - 1)
                        STT(sqb[:, c % 2, :], x[:, c, :], prm(gain, c), rstd[:, :], M, M).then_inc(s_ht, 1)
                    if c:
                        ve.wait_ge(s_hhi, base + c)
                        ve.wait_ge(s_ht, base + c)
                        TT(hl[:, c - 1, :], sqb[:, (c - 1) % 2, :], hh[:, c - 1, :].bitcast(F32), SU).then_inc(s_h, 1)
                hmade[0] += 1

            def norm():
                ve.wait_ge(s_root, norms[0] + 1)
                norms[0] += 1

            def derive():
                mu, ka = POFF["rwkv_mu"], POFF["rwkv_k_a"]
                TS(dpar[:, 0:8], par[:, mu:mu + 8], -1.0, 1.0, M, AD)
                TS(dpar[:, 8:16], par[:, mu:mu + 8], 0.5, None, M)
                TS(dpar[:, 16:18], par[:, ka:ka + 2], -1.0, 1.0, M, AD)
                b1 = POFF["hy_ff_b1"]
                step(TS(dpar[:, 18:20], par[:, b1:b1 + 2], prm("hy_sin_freq"), None, M))

            def add_out(l, part, v, factor, banks):
                n = x_count(l, part) + v
                ve.wait_ge(s_fo, n + 1)
                if n >= 16 and (part, v) != (0, 0):
                    ve.wait_ge(s_xup, n - 15)
                xs = x[:, (v // 2) % KT, (v % 2) * HALF:(v % 2 + 1) * HALF]
                STT(xs, bank(banks + v % 4, HALF), factor, xs, M, AD).then_inc(s_xup, 1)

            def ffn(l, f, cap):
                n = use_base(l, 3 if f else 0)
                for b, (j0, nj) in enumerate(FF_BLOCKS):
                    for j in range(j0, j0 + nj):
                        split_to(min(n + 3, cap))
                        n += 2
                        for hf_ in range(2):
                            u = (2 * l + f) * 2 * FT + 2 * j + hf_
                            ve.wait_ge(s_silu, u + 1)
                            if u >= 2:
                                ve.wait_ge(s_act, u - 1)
                            TT(gated[:, u % 2, :], silu[:, u % 2, :], bank(2 * (u % 2) + 1, HALF), M).then_inc(s_mul, 1)
                            ve.wait_ge(s_ahi, u + 1)
                            cols = slice(hf_ * HALF, (hf_ + 1) * HALF)
                            TT(al_[:, j - j0, cols], gated[:, u % 2, :], ah[:, j - j0, cols].bitcast(F32), SU)\
                                .then_inc(s_act, 1)
                    for m in range(OUT_TILES):
                        split_to(min(n + 2, cap))
                        n += 1
                        for hf_ in range(2):
                            add_out(l, f, 16 * b + 2 * m + hf_, 0.5, 4)
                        if b == 2 and m:
                            add_squares(m - 1)
                add_squares(OUT_TILES - 1)

            def zero_pads(bufs):
                for b in bufs:
                    for c in (0, SEQ + 1, T + 2):
                        m = ve.memset(b[:, c:c + 1], 0.0)
                m.then_inc(s_zero, 1)

            def shift_mix(l, i, cap):
                pi = 14 * l + i
                split_to(min(use_base(l, 1) + i + 2, cap))
                b = raw[pi % 2]
                ve.wait_ge(s_raw, 2 * pi + 2)
                step(TT(nbr[:, :], b[:, 0:T + 1], b[:, 2:T + 3], AD))
                step(TS(nbr[:, :], nbr[:, :], dpar[:, 8 + i:9 + i], None, M))
                for s, (t0, tn) in enumerate(SEGS):
                    m = STT(pa[:, i, t0:t0 + tn], b[:, 1 + t0 + s:1 + t0 + s + tn], dpar[:, i:i + 1],
                            nbr[:, t0 + s:t0 + s + tn], M, AD)
                m.then_inc(s_mixd, 1)
                ve.wait_ge(s_mixd, pi + 1)

            def conv_mix(l, i, cap):
                pi = 14 * l + A_TILES + i
                split_to(min(use_base(l, 1) + A_TILES + i + 2, cap))
                b = hraw[pi % 2]
                ve.wait_ge(s_raw, 2 * pi + 2)
                step(TS(hnb[:, :], b[:, 1:T + 2], prm("hy_conv_w", 6 + i), prm("hy_conv_b", i), M, AD))
                step(STT(hnb[:, :], b[:, 0:T + 1], prm("hy_conv_w", i), hnb[:, :], M, AD))
                for s, (t0, tn) in enumerate(SEGS):
                    m = STT(conv[:, i, t0:t0 + tn], b[:, 2 + t0 + s:2 + t0 + s + tn], prm("hy_conv_w", 12 + i),
                            hnb[:, t0 + s:t0 + s + tn], M, AD)
                m.then_inc(s_mixd, 1)
                ve.wait_ge(s_mixd, pi + 1)

            def flat(t):
                return t.rearrange("p c t -> p (c t)")

            def batch(l, d, i, s, f):
                k, o = (l, "b", d, i), 4 * f
                masks = ((LOW_D, LOW_O, LOW_S, LOW_I), (UP_D, UP_O, UP_S, UP_I))
                low, up = masks if d == 0 else masks[::-1]
                cp = ve.tensor_copy
                h = slice(f * HB, (f + 1) * HB)
                half = lambda t: t[:, h, :].rearrange("p (b c) t -> p b c t", b=2)
                q3 = lambda a: Q[f][:, :, a, :].rearrange("p (b c) t -> p b c t", b=2)
                r3 = lambda a: R[:, h, a, :].rearrange("p (b c) t -> p b c t", b=2)

                def diagonal(dst, src, blocks=BLOCKS):
                    for r, a in blocks:
                        m = cp(dst[r, h, a, :], src[r, :, :])
                    return m

                ve.wait_ge(*rp.at(*k, s, f))
                if s:
                    ve.wait_ge(*rv.at(*k, s - 1, f))
                if s == 0:
                    TT(Na[:, h, :], units(o), mask(low[0]), M)
                    w1 = wide_units(o + 1)
                    TT(half(Ma), w1[:, :, :, 0, :], mask3(up[0]), M)
                    TT(No[:, h, :], units(o), mask(low[1]), M)
                    m = TT(half(Mrb), w1[:, :, :, 1, :], mask3(up[3]), M)
                elif s == 1:
                    w3 = wide_units(o)
                    for r, a in BLOCKS:
                        dst = Lak_bd[r, h, a, :].rearrange("p (b c) t -> p b c t", b=2)
                        TT(dst, w3[r, :, :, 0, :], mask3(up[2])[r], M)
                    TT(X[:, h, :], Ma[:, h, :], eye_b(), AD)
                    m = TT(half(Mrk), w3[:, :, :, 1, :], mask3(up[3]), M)
                elif s == 2:
                    diagonal(Mb_bd, units(o + 2))
                    m = cp(Mb[:, h, :], units(o + 2))
                elif s == 3:
                    w = wide_units(o + 2)
                    for r, a in BLOCKS:
                        cp(Ma_bd[r, h, a, :].rearrange("p (b c) t -> p b c t", b=2), w[r, :, :, 0, :])
                    m = TT(half(X), half(X), w[:, :, :, 1, :], AD)
                elif s == 4:
                    m = TT(X[:, h, :], X[:, h, :], units(o), AD)
                elif s == 5:
                    TT(X[:, h, :], X[:, h, :], units(o), AD).then_inc(*rv.inc(l, "first", d, i, s, f))
                    ve.wait_ge(*rv.at(l, "first", d, i, s, f))
                    m = diagonal(X_bd, X[:, h, :], BLOCKS[:1])
                elif s == 6:
                    diagonal(Na_bd, units(o + 1))
                    m = cp(Ma[:, h, :], units(o))
                elif s == 7:
                    m = diagonal(Mb_bd, units(o), BLOCKS[:1])
                elif s == 8:
                    w = wide_units(o)
                    for a in range(2):
                        m = TT(r3(a), q3(a), w[:, :, :, a, :], AD)
                elif s == 9:
                    w = wide_units(o + 2)
                    TT(q3(1), r3(1), w[:, :, :, 1, :], AD).then_inc(*rv.inc(l, "first", d, i, s, f))
                    for r, a in BLOCKS:
                        dst = Q0_bd[r, h, a, :].rearrange("p (b c) t -> p b c t", b=2)
                        m = TT(dst, r3(0)[r], w[r, :, :, 0, :], AD)
                else:
                    w = wide_units(o)
                    eye = cs("eye").unsqueeze(1).unsqueeze(1).broadcast_to([P, 2, HB // 2, CH])
                    halves = lambda t: half_cols(t, i, f).rearrange("p (b c) t -> p b c t", b=2)
                    TT(halves(trans), w[:, :, :, 0, :], eye, AD)
                    decay_end = pc[:, i, h].unsqueeze(2).broadcast_to([P, HB, CH])
                    TT(half_cols(inject, i, f), units(o + 2), decay_end, M)
                    rho = ar[:, h, 1, :].rearrange("p (b c) t -> p b c t", b=2)
                    m = TT(halves(query), w[:, :, :, 1, :], rho, AD)
                m.then_inc(*rv.inc(*k, s, f))

            def cumulate(l, d, i):
                ve.wait_ge(*ra_.at(l, "sig", d, i))
                step(TS(tmp[:, 0, :], tmp[:, 0, :], DECAY_SCALE, None, M))
                if d == 0:
                    step(ve.tensor_tensor_scan(tmp[:, 2, :], scanm[:, 0:T], tmp[:, 0, :], 0.0, M, AD))
                else:
                    step(ve.tensor_tensor_scan(tmp[:, 2, ::-1], scanm[:, T:0:-1], tmp[:, 0, ::-1], 0.0, M, AD))
                TT(tmp[:, 0, :], tmp[:, 2, :], tmp[:, 0, :], SU).then_inc(*rv.inc(l, "cum", d, i))

            def keys(l, d, i):
                kf, bf, k_in = flat(kap[:, :, :]), flat(beta[:, :, :]), pa[:, 2 + i, :]
                step(TS(kf, tmp[:, 1, :], prm("rwkv_k_a", i), dpar[:, 16 + i:17 + i], M, AD))
                step(TT(kf, kf, k_in, M))
                if d == 0:
                    ve.tensor_copy(ksum[:, i, :], kf)
                else:
                    TT(ksum[:, i, :], ksum[:, i, :], kf, AD)
                TT(bf, kk[:, i, :], tmp[:, 1, :], M).then_inc(*rv.inc(l, "keys", d, i))

            def features(l, d, i):
                v3 = lambda t: t.rearrange("p (c t) -> p c t", t=CH)
                ve.wait_ge(*rv.at(l, "keys", d, i))
                ve.wait_ge(*ra_.at(l, "expE", d, i))
                TT(ar[:, :, 0, :], v3(kk[:, i, :]), v3(tmp[:, 0, :]), M).then_inc(*rv.inc(l, "alpha", d, i))
                ve.wait_ge(*ra_.at(l, "expN", d, i))
                TT(beta[:, :, :], beta[:, :, :], v3(tmp[:, 2, :]), M).then_inc(*rv.inc(l, "beta", d, i))
                if (d, i) == (0, 0):
                    ve.wait_ge(s_clear, l + 1)
                ve.wait_ge(*ra_.at(l, "expL", d, i))
                TT(ar[:, :, 1, :], v3(pa[:, i, :]), v3(tmp[:, 3, :]), M)
                ve.tensor_copy(pc[:, i, :], v3(tmp[:, 3, :])[:, :, CH - 1 if d == 0 else 0])
                for r, a in BLOCKS:
                    m = TT(kap_bd[r, :, a, :], kap[r, :, :], v3(tmp[:, 2, :])[r], M)
                m.then_inc(*rv.inc(l, "feat", d, i))

            def rwkv(l):
                step(ve.memset(scanm[:, :], 1.0))
                step(ve.memset(scanm[:, 0:T + 1:CH], 0.0))
                for i in range(2):
                    step(TS(tmp[:, 0, :], pa[:, 2 + i, :], prm("rwkv_k_k", i), None, M))
                    TT(tmp[:, 1, :], tmp[:, 0, :], tmp[:, 0, :], M).then_inc(*rv.inc(l, "ksq", i))
                    ve.wait_ge(*rp.at(l, "ksq", i))
                    for s, (t0, tn) in enumerate(SEGS):
                        m = TS(tmp[:, 2, t0:t0 + tn], bank(s, tn), 1e-24 / HD, None, ALU.max)
                    m.then_inc(*rv.inc(l, "kmax", i))
                    ve.wait_ge(*rp.at(l, "vt", i))
                    for f in range(2):
                        m = ve.tensor_copy(half_cols(vtok, i, f), units(2 + f))
                    m.then_inc(*rv.inc(l, "vt", i))
                    ve.wait_ge(*ra_.at(l, "kroot", i))
                    TT(kk[:, i, :], tmp[:, 0, :], tmp[:, 2, :], M).then_inc(*rv.inc(l, "kk", i))
                    ve.wait_ge(*rv.at(l, "kk", i))
                for d in range(2):
                    cumulate(l, d, 0)
                    keys(l, d, 0)
                    for i in range(2):
                        if i:
                            ve.wait_ge(*rv.at(l, "b", d, 0, BATCH - 1, 1))
                        features(l, d, i)
                        ve.wait_ge(*rv.at(l, "feat", d, i))
                        for s in range(BATCH):
                            for f in range(2):
                                batch(l, d, i, s, f)
                                if (i, s, f) == (0, 8, 1):
                                    cumulate(l, d, 1)
                                if (i, s, f) == (0, 9, 1):
                                    keys(l, d, 1)
                    ve.wait_ge(*rv.at(l, "b", d, 1, BATCH - 1, 1))
                    for s in range(1, 8):
                        if s == 1:
                            for c, col in chain(d, 0):
                                ve.memset(state[:, :, c, :], 0.0)
                        else:
                            ve.wait_ge(*rp.at(l, "chain", d, s))
                        prev = chain(d, s - 1)
                        for c, col in chain(d, s):
                            pcol = [p for p, q in prev if q == col][0]
                            if s == 1:
                                m = ve.tensor_copy(state[:, :, c, :], inject[:, :, pcol, :])
                            else:
                                got = ps[:, 0, 0:256].rearrange("p (i q t) -> p i q t", i=2, q=2)[:, :, col, :]
                                de = pc[:, :, pcol].unsqueeze(2).broadcast_to([P, 2, CH])
                                step(TT(state[:, :, c, :], got, de, M))
                                m = TT(state[:, :, c, :], state[:, :, c, :], inject[:, :, pcol, :], AD)
                        m.then_inc(*rv.inc(l, "state", d, s))
                    for i in range(2):
                        ve.wait_ge(*rp.at(l, "read", d, i))
                        ve.wait_ge(*ra_.at(l, "b", d, i, BATCH - 1, 1))
                        for f in range(2):
                            m = TT(half_cols(olocal, i, f), half_cols(olocal, i, f), units(2 * i + f), AD)
                        m.then_inc(*rv.inc(l, "oread", d, i))
                    for i in range(2):
                        ve.wait_ge(*rp.at(l, "mean", d, i))
                        ve.wait_ge(*rv.at(l, "oread", d, i))
                        for f in range(2):
                            m = TT(half_cols(olocal, i, f), half_cols(olocal, i, f), units(4 + 2 * i + f), SU)
                        m.then_inc(*rv.inc(l, "ocen", d, i))
                    for i in range(2):
                        ve.wait_ge(*ra_.at(l, "oroot", d, i))
                        o = flat(olocal[:, i, :, :])
                        step(TT(o, o, tmp[:, 2 * i + 1, :], M))
                        if d == 0:
                            m = TS(mixed[:, i, :], o, prm("rwkv_ln_g", i), prm("rwkv_ln_b", i), M, AD)
                        else:
                            step(TS(o, o, prm("rwkv_ln_g", i), prm("rwkv_ln_b", i), M, AD))
                            m = TT(mixed[:, i, :], mixed[:, i, :], o, AD)
                        m.then_inc(*rv.inc(l, "onorm", d, i))
                for i in range(2):
                    ve.wait_ge(*rv.at(l, "onorm", 1, 1))
                    TT_in = STT(tmp[:, 0, :], pa[:, i, :], prm("rwkv_r_k", i), ksum[:, i, :], M, M)
                    TT_in.then_inc(*rv.inc(l, "rk", i))
                    ve.wait_ge(*rp.at(l, "bonus", i))
                    for s, (t0, tn) in enumerate(SEGS):
                        step(STT(tmp[:, 1, t0:t0 + tn], bank(s, tn), float(HD), pa[:, 4 + i, t0:t0 + tn], M, M))
                    step(TT(mixed[:, i, :], mixed[:, i, :], tmp[:, 1, :], AD))
                    for s, (t0, tn) in enumerate(SEGS):
                        m = TT(mixed[:, i, t0:t0 + tn], mixed[:, i, t0:t0 + tn], bank(2 + s, tn), M)
                    m.then_inc(*rv.inc(l, "done", i))

            def gn(tile, gain, c):
                ve.wait_ge(s_g3, gns[0] + 1)
                STT(mixed[:, tile, :], mixed[:, tile, :], prm(gain, c), sqb[:, gns[0] % 2, :], M, M).then_inc(s_g4, 1)
                gns[0] += 1

            def reduce_arg(l, n, column):
                ve.wait_ge(*hp.at(l, f"f{n}"))
                for s, (t0, tn) in enumerate(SEGS):
                    m = TS(arg[0:64, t0:t0 + tn], ps[0:64, s, 0:tn], prm("hy_sin_freq", 0, 64), dpar[0:64, column:column + 1], M, AD)
                step(m)
                a, r = arg[0:64, :], h1[0:64, :]
                step(TS(r, a, float(1 / (2 * np.pi)), MAGIC, M, AD))
                step(TS(r, r, -MAGIC, None, AD))
                step(STT(a, r, -TWO_PI_HI, a, M, AD))
                step(STT(a, r, -TWO_PI_LO, a, M, AD))
                TS(a, a, PI, -PI, ALU.min, ALU.max).then_inc(*hv.inc(l, f"a{n}"))

            def filters(l):
                reduce_arg(l, 1, 18)
                reduce_arg(l, 2, 19)
                for p in range(6):
                    ve.wait_ge(*hp.at(l, "f3", p))
                    if p:
                        ve.wait_ge(*hv.at(l, "eo", p - 1))
                    win = hdecay[:, p, :].unsqueeze(1).broadcast_to([P, 2, 256])
                    o2 = lambda t: t.rearrange("p (o c) -> p o c", o=2)
                    TT(o2(hf[:, :]), o2(bank(4 * (p % 2))), win, M)
                    m = TT(o2(hb[:, :]), o2(bank(4 * (p % 2) + 1)), win, M)
                    if p in (0, 4):
                        step(m)
                        m = ve.memset(hb[0:1, :], 0.0)
                    m.then_inc(*hv.inc(l, "win", p))
                    ve.wait_ge(*hv.at(l, "win", p))
                    TT(se[:, p, :], hf[:, :], hb[:, :], AD)
                    m = TT(so[:, p, :], hf[:, :], hb[:, :], SU)
                    m.then_inc(*hv.inc(l, "eo", p))
                    ve.wait_ge(*ha.at(l, "abs", p))
                ve.wait_ge(*hp.at(l, "fabs", 5))
                for s in range(2):
                    m = ve.reciprocal(nrm[:, s, :], bank(6 + s))
                m.then_inc(*hv.inc(l, "norm"))
                ve.wait_ge(*hv.at(l, "norm"))
                ve.wait_ge(*ha.at(l, "skip"))
                for ft in range(6):
                    s = 0 if ft < 4 else 1
                    wf = cst[:, COFF["wf"] + ft:COFF["wf"] + ft + 1]
                    ve.wait_ge(*hp.at(l, "kern", ft))
                    TT(kcos[:, ft, :], bank(4 * (ft % 2)), nrm[:, s, :], M)
                    m = TT(ksin[:, ft, :], bank(4 * (ft % 2) + 1), nrm[:, s, :], M)
                    if ft in (0, 4):
                        m = TT(knyq[0:1, s, :], ps[0:1, 2, :], nrm[0:1, s, :], M)
                    step(m)
                    TS(ksin[:, ft, :], ksin[:, ft, :], wf, None, M)
                    m = TT(kcos[:, ft, :], kcos[:, ft, :], skipb[:, :], AD)
                    if ft in (0, 4):
                        m = TT(knyq[0:1, s, :], knyq[0:1, s, :], skipb[0:1, :], AD)
                    step(m)
                    m = TS(kcos[:, ft, :], kcos[:, ft, :], wf, None, M)
                    if ft in (0, 4):
                        m = TS(knyq[0:1, s, :], knyq[0:1, s, :], 0.5 / (SEQ, DEC)[s], None, M)
                    m.then_inc(*hv.inc(l, "kern", ft))

            def hyena(l):
                for g in range(6):
                    ve.wait_ge(*hp.at(l, "tr", g))
                    ve.tensor_copy(vt[:, g, :], ps[:, 4 + g % 2, 0:256])
                    ve.tensor_copy(x1t[:, g, :], ps[:, 4 + g % 2, 256:512]).then_inc(*hv.inc(l, "tr", g))
                for o in range(2):
                    kcol = slice(256 * o, 256 * o + 256)
                    for ft in range(6):
                        ve.wait_ge(*hp.at(l, "dft", o, ft))
                        if ft:
                            ve.wait_ge(*hv.at(l, "dft", o, ft - 1))
                        xc, xs = ps[:, ft % 2, 0:256], ps[:, ft % 2, 256:512]
                        TT(prod[:, 0, :], xc, kcos[:, ft, kcol], M)
                        TT(prod[:, 1, :], xs, ksin[:, ft, kcol], M)
                        TT(prod[:, 2, :], xc, ksin[:, ft, kcol], M)
                        m = TT(prod[:, 3, :], xs, kcos[:, ft, kcol], M)
                        if ft in (0, 4):
                            s = ft // 4
                            m = TT(xnyq[0:1, s, :], ps[0:1, 2, 0:256], knyq[0:1, s, kcol], M)
                        step(m)
                        TT(yc[:, ft, :], prod[:, 0, :], prod[:, 1, :], SU)
                        TT(ys[:, ft, :], prod[:, 2, :], prod[:, 3, :], AD).then_inc(*hv.inc(l, "dft", o, ft))
                    if o == 0:
                        for tt in range(6):
                            ve.wait_ge(*hp.at(l, "inv", 0, tt))
                            TT(zt[:, tt, :], x1t[:, tt, :], ps[:, 4 + tt % 2, 0:256], M).then_inc(*hv.inc(l, "inv", 0, tt))
                    else:
                        for i in range(2):
                            ve.wait_ge(*hp.at(l, "inv", 1, i))
                            for s, (t0, tn) in enumerate(SEGS):
                                m = TT(mixed[:, 6 + i, t0:t0 + tn], conv[:, 4 + i, t0:t0 + tn], bank(4 + s, tn), M)
                            m.then_inc(*hv.inc(l, "inv", 1, i))
                for i in range(2):
                    gn(6 + i, "hy_out_norm", i)

            def attention(l):
                for g in range(16):
                    ve.wait_ge(s_bp, 16 * l + g + 1)
                    src = ps[:, 4 + g % 2, 0:480].rearrange("p (k h d) -> p h d k", k=4, h=8)
                    cm = COFF["colmask"] + 4 * g
                    for half in range(2):
                        r = slice(64 * half, 64 * half + 64)
                        for hd in range(8):
                            m = TT(bias[r, hd, half:half + 15, 4 * g:4 * g + 4], src[r, hd, :, :],
                                   cst[r, cm:cm + 4].unsqueeze(1).broadcast_to([64, 15, 4]), AD)
                    m.then_inc(s_bv, 1)

                def smooth(u):
                    hd, i = u // 6, u % 6
                    kn, rows, top = (512, 8, 7 - 2 * i) if i < 4 else (256, 4, 7 - 2 * (i - 4))
                    n = 48 * l + u
                    ve.wait_ge(s_sc, n + 1)
                    if n >= SCB:
                        ve.wait_ge(s_tr, n - SCB + 1)
                    g = sc[:, u % SCB, 0:kn]
                    step(STT(g.rearrange("p (r c) -> p r c", c=64), bank(u % 2, kn).rearrange("p (r c) -> p r c", c=64),
                             HD ** -0.5, bias[:, hd, top:top + rows, :], M, AD))
                    ve.tensor_reduce(nmax[:, u % SCB:u % SCB + 1], g, AX.X, ALU.max, negate=True).then_inc(s_sm, 1)

                def normed(u):
                    kn = 512 if u % 6 < 4 else 256
                    ve.wait_ge(s_pr, 48 * l + u + 1)
                    b = u % SCB
                    step(ve.reciprocal(rsum[:, b:b + 1], ssum[:, b:b + 1]))
                    TS(sc[:, b, 0:kn], sc[:, b, 0:kn], rsum[:, b:b + 1], None, M).then_inc(s_pn, 1)

                ve.wait_ge(s_bv, 16 * (l + 1))
                for u in range(48 + LAG - 1):
                    if u < 48:
                        smooth(u)
                    if u >= LAG - 1:
                        normed(u - LAG + 1)
                for i in range(4):
                    gn(2 + i, "na_out_norm", i)

            def mix_out(l):
                for k in range(OUT_TILES):
                    if k == 1:
                        split_to(use_base(l, 2))
                    ve.wait_ge(s_mhi, 8 * l + k + 1)
                    TT(ml[:, k, :], mixed[:, k, :], mh[:, k, :].bitcast(F32), SU).then_inc(s_m, 1)
                for m in range(OUT_TILES):
                    split_to(use_base(l, 2) + m + 2)
                    for f in range(2):
                        add_out(l, 2, 2 * m + f, 1.0, 0)
                    if m:
                        add_squares(m - 1)
                add_squares(OUT_TILES - 1)

            ve.memset(eps[:, 0:1], NORM_EPS)
            ve.memset(eps[:, 2:3], 0.0)
            ve.memset(eps[:, 1:2], GN_EPS).then_inc(s_eps, 1)
            ve.wait_ge(s_x, 16)
            ve.wait_ge(s_const, 16)
            for m in range(OUT_TILES):
                add_squares(m)
            for l in L:
                ve.wait_ge(s_par, 32 * (l + 1))
                cap_a = use_base(l, 1) + A_TILES - 1
                cap_b = use_base(l, 2) - 1
                derive()
                norm()
                split_to(use_base(l, 0) + 1)
                split_h("norm_ffn1")
                ffn(l, 0, cap_a)
                norm()
                split_h("norm_mix")
                zero_pads(raw)
                for i in range(A_TILES):
                    shift_mix(l, i, cap_a)
                rwkv(l)
                split_to(use_base(l, 1) + A_TILES)
                ve.wait_ge(s_back, 16 * (l + 1))
                split_h("norm_mix")
                zero_pads(hraw)
                for i in range(C_TILES):
                    conv_mix(l, i, cap_b)
                for i in range(QK_TILES):
                    split_to(min(use_base(l, 1) + A_TILES + C_TILES + i + 2, cap_b))
                split_to(cap_b)
                ve.wait_ge(s_qkc, 14 * (l + 1))
                attention(l)
                ve.wait_ge(s_hz, 48 * (l + 1))
                filters(l)
                hyena(l)
                mix_out(l)
                norm()
                split_h("norm_ffn2")
                ffn(l, 1, LAYERS * USES)
            norm()
            for c in range(KT):
                m = STT(hout[:, c, :], x[:, c, :], prm("final_norm", c), rstd[:, :], M, M)
            m.then_inc(s_fin, 1)


def constants():
    c = np.zeros((P, NCONST), np.float32)
    p = np.arange(P)
    row, col = (p % CH)[:, None], np.arange(CH)[None, :]

    def put(name, v):
        c[0:v.shape[0], COFF[name]:COFF[name] + v.shape[1]] = v

    put("ident", np.eye(P))
    put("ones", np.ones((P, P)))
    put("blk", (p[:, None] // HD == p[None, :] // HD) / float(HD))
    low, up, same = col < row, col > row, col // 16 == row // 16
    put("masks", np.concatenate([-1.0 * (low & same), -1.0 * (low & ~same), -1.0 * (up & same), -1.0 * (up & ~same),
                                 1.0 * low, 1.0 * up, 1.0 * (col <= row), 1.0 * (col >= row)], 1))
    put("eye", 1.0 * (col == row))
    put("alt", (1.0 - 2.0 * (p % 2))[:, None])
    wf = np.zeros((P, 6))
    for ft in range(6):
        n = SEQ if ft < 4 else DEC
        wf[:, ft] = 1.0 / n
    wf[0, 0], wf[0, 4] = 0.5 / SEQ, 0.5 / DEC
    put("wf", wf)
    m = np.arange(P)
    put("shift", 1.0 * (np.arange(31)[:, None] == 78 - m[None, :]))
    qc, kc = (p % GRID)[:, None], np.arange(GRID)[None, :]
    start = np.clip(qc - 8, 0, GRID - 16)
    put("colmask", np.where((kc >= start) & (kc < start + 16), 0.0, NEG))
    return c


def hyena_constants():
    c = np.zeros((P, NHY), np.float32)
    n = np.arange(512)
    ang = 2 * np.pi * ((n[:, None] * n[None, :]) % 1024) / 1024.0
    rows = lambda a: a.reshape(4, P, 512).transpose(1, 0, 2).reshape(P, 2048)
    c[:, HOFF["cos"]:HOFF["cos"] + 2048] = rows(np.cos(ang))
    c[:, HOFF["sin"]:HOFF["sin"] + 2048] = rows(np.sin(ang))
    deltas = np.abs(np.linspace(np.log(1e-2) / 1.5, np.log(1e-2) / 0.3, C_DIM))
    for s, (t0, tn) in enumerate(SEGS):
        t = np.linspace(0.0, 1.0, tn)
        dec = np.exp(-t[:, None] * deltas[None, :]).reshape(tn // P, P, C_DIM).transpose(1, 0, 2)
        o = HOFF["decay"] + 256 * (t0 // P)
        c[:, o:o + 256 * (tn // P)] = dec.reshape(P, -1)
        w = 2 * np.pi * np.arange(tn) / tn
        f = np.linspace(1e-4, 15, 16)
        fw = f[:, None] * w[None, :]
        z = np.concatenate([t[None, :], np.cos(fw), -np.sin(fw)], 0)
        c[0:33, HOFF["z"] + t0:HOFF["z"] + t0 + tn] = z
    c[:, HOFF["altrow"]:HOFF["altrow"] + 512] = 1.0 - 2.0 * (n % 2)
    return c


def pack(inputs):
    a = {k: np.ascontiguousarray(v) for k, v in inputs.items()}
    x = np.concatenate([a["x_prompt"][0], a["x_sample"][0]], 0)
    out = {"xT": np.ascontiguousarray(x.T.reshape(KT, P, T).transpose(1, 0, 2))}

    def tiles(w):
        k, n = w.shape
        return w.reshape(k // P, P, n // P, P).transpose(2, 1, 0, 3).reshape(n // P, P, -1)

    wa, par, small, hw = [], [], [], []
    for l in range(LAYERS):
        def ffn(w_in, w_out):
            t, parts = tiles(w_in), []
            for j0, nj in FF_BLOCKS:
                parts.append(np.stack([t[j0:j0 + nj], t[FT + j0:FT + j0 + nj]], 1).reshape(2 * nj, P, -1))
                o = tiles(w_out[P * j0:P * (j0 + nj)])
                parts.append(np.concatenate([o, np.zeros((OUT_TILES, P, KT * P - o.shape[2]), np.float32)], 2))
            return np.concatenate(parts, 0)
        w = a["w_in"][l]
        gate_pad = np.concatenate([w[:, 896:960], np.zeros((D, 64), np.float32)], 1)
        wp = np.concatenate([w[:, 0:896], gate_pad, w[:, 960 + 1536:], w[:, 960:960 + 1536]], 1)
        wa.append(np.concatenate([ffn(a["ffn1_w_in"][l], a["ffn1_w_out"][l]), tiles(wp), tiles(a["w_out"][l]),
                                  ffn(a["ffn2_w_in"][l], a["ffn2_w_out"][l])], 0))
        pr = np.zeros((P, NPAR), np.float32)
        for name, n in PCOLS:
            v = (a[name] if name == "final_norm" else a[name][l]).reshape(-1)
            if v.size < n * P:
                v = np.concatenate([v, np.zeros(n * P - v.size, np.float32)])
            pr[:, POFF[name]:POFF[name] + n] = v.reshape(n, P).T
        par.append(pr)
        sm = np.zeros((P, NSMALL), np.float32)
        sm[:, SOFF["lora"]:SOFF["lora"] + 256] = np.concatenate(
            [a["rwkv_w_up"][l].reshape(64, 256), a["rwkv_a_up"][l].reshape(64, 256)], 0)
        sm[0:64, SOFF["g_up"]:SOFF["g_up"] + 256] = a["rwkv_g_up"][l]
        sm[0:31, SOFF["rpb"]:SOFF["rpb"] + 120] = a["na_rpb"][l].transpose(2, 0, 1).reshape(31, 120)
        small.append(sm)
        hh = np.zeros((P, NHW), np.float32)
        hh[0:33, 0:64] = a["hy_ff_w1"][l]
        hh[0:64, 64:128] = a["hy_ff_w2"][l]
        hh[0:64, 128:1152] = a["hy_ff_w3"][l]
        hh[0:1, 1152:1664] = a["hy_bias"][l].reshape(1, 512)
        hw.append(hh)
    out.update(wa=np.stack(wa), par=np.stack(par), small=np.stack(small),
               const=constants(), hyc=hyena_constants(), hyw=np.stack(hw))
    return out


def kernel(**inputs):
    import concourse.bacc as _bacc
    from concourse.bass_utils import run_bass_kernel_spmd as _run

    arrays = pack(inputs)
    nc = _bacc.Bacc("TRN2", target_bir_lowering=False, num_devices=1)
    args = [nc.dram_tensor(n, v.shape, mybir.dt.from_np(v.dtype), kind="ExternalInput").ap() for n, v in arrays.items()]
    args.append(nc.dram_tensor("outT", (P, KT, T), F32, kind="ExternalOutput").ap())
    build(nc, *args)
    r = _run(nc, [arrays], core_ids=[0])
    y = r.results[0]["outT"].transpose(2, 1, 0).reshape(T, D)
    return np.ascontiguousarray(y[:SEQ][None]), np.ascontiguousarray(y[SEQ:][None])
```
